# Optimizing a Trainium2 kernel written in Bass

```python
import jax, jax.numpy as jnp
from jax import lax
import numpy as np

D_MODEL = 2048
BATCH = 1
SEQ = 256
DEPTH = 1

N_MEM = 256
WIDTH_A = D_MODEL
WIDTH_B = D_MODEL
MIX_WIDTH = WIDTH_A + WIDTH_B
HEAD_DIM = 128
N_HEADS_B = WIDTH_B // HEAD_DIM
CONV_WIDTH_A = 3
CONV_WIDTH_B = 4
LRU_C = 8.0
XATTN_HEADS = 4
XATTN_HEAD_DIM = D_MODEL // XATTN_HEADS
IN_COLS = 4 * WIDTH_A + 2 * WIDTH_B
RMS_EPS = 1e-6

kernel_name = "hymba_shortconv_rglru_memxattn"

def rms_norm(x, g):
    xf = x.astype(jnp.float32)
    y = xf * lax.rsqrt(jnp.mean(xf * xf, axis=-1, keepdims=True) + RMS_EPS)
    return (y * g.astype(jnp.float32)).astype(x.dtype)

def causal_depthwise_conv(u, w, b):
    k_width = w.shape[0]
    s = u.shape[1]
    up = jnp.pad(u, ((0, 0), (k_width - 1, 0), (0, 0)))
    y = b
    for k in range(k_width):
        y = y + up[:, k:k + s] * w[k]
    return y

def _lin_rec_combine(c1, c2):
    a1, b1 = c1
    a2, b2 = c2
    return a1 * a2, a2 * b1 + b2

def rg_lru(xc, w_r, b_r, w_i, b_i, lam):
    bsz, s, _ = xc.shape
    xh = xc.reshape(bsz, s, N_HEADS_B, HEAD_DIM)
    r_pre = jnp.einsum('bshi,hij->bshj', xh, w_r).reshape(bsz, s, WIDTH_B) + b_r
    i_pre = jnp.einsum('bshi,hij->bshj', xh, w_i).reshape(bsz, s, WIDTH_B) + b_i
    r = jax.nn.sigmoid(r_pre.astype(jnp.float32))
    i = jax.nn.sigmoid(i_pre.astype(jnp.float32))
    log_a = -LRU_C * r * jax.nn.softplus(-lam.astype(jnp.float32))
    a = jnp.exp(log_a)
    mult = jnp.sqrt(-jnp.expm1(2.0 * log_a))
    mult = mult.at[:, 0].set(1.0)
    u = mult * i * xc.astype(jnp.float32)
    _, h = lax.associative_scan(_lin_rec_combine, (a, u), axis=1)
    return h.astype(xc.dtype)

def memory_cross_attention(hn, mn, w_q, w_kv, w_o):
    bsz, s, _ = hn.shape
    m = mn.shape[1]
    q = (hn @ w_q).reshape(bsz, s, XATTN_HEADS, XATTN_HEAD_DIM)
    kv = mn @ w_kv
    k = kv[..., :D_MODEL].reshape(bsz, m, XATTN_HEADS, XATTN_HEAD_DIM)
    v = kv[..., D_MODEL:].reshape(bsz, m, XATTN_HEADS, XATTN_HEAD_DIM)
    scores = jnp.einsum('bshd,bmhd->bhsm', q, k).astype(jnp.float32) * (XATTN_HEAD_DIM ** -0.5)
    p = jax.nn.softmax(scores, axis=-1).astype(v.dtype)
    o = jnp.einsum('bhsm,bmhd->bshd', p, v).reshape(bsz, s, D_MODEL)
    return o @ w_o

def setup_inputs(seed: int = 0) -> dict:
    key = jax.random.key(seed)
    ks = jax.random.split(key, 24)
    f32 = jnp.float32
    nrm = lambda k, shape, scale: jax.random.normal(k, shape, f32) * scale
    a_base = jax.random.uniform(ks[10], (DEPTH, WIDTH_B), f32, 0.9, 0.999)
    return {
        "x": nrm(ks[0], (BATCH, SEQ, D_MODEL), 1.0),
        "mem": nrm(ks[1], (BATCH, N_MEM, D_MODEL), 1.0),
        "norm_mix_g": 1.0 + nrm(ks[2], (DEPTH, D_MODEL), 0.02),
        "w_in": nrm(ks[3], (DEPTH, D_MODEL, IN_COLS), D_MODEL ** -0.5),
        "conv_a_w": nrm(ks[4], (DEPTH, CONV_WIDTH_A, WIDTH_A), CONV_WIDTH_A ** -0.5),
        "conv_a_b": nrm(ks[5], (DEPTH, WIDTH_A), 0.01),
        "conv_b_w": nrm(ks[6], (DEPTH, CONV_WIDTH_B, WIDTH_B), CONV_WIDTH_B ** -0.5),
        "conv_b_b": nrm(ks[7], (DEPTH, WIDTH_B), 0.01),
        "w_rgate": nrm(ks[8], (DEPTH, N_HEADS_B, HEAD_DIM, HEAD_DIM), HEAD_DIM ** -0.5),
        "b_rgate": nrm(ks[9], (DEPTH, WIDTH_B), 0.01),
        "w_igate": nrm(ks[11], (DEPTH, N_HEADS_B, HEAD_DIM, HEAD_DIM), HEAD_DIM ** -0.5),
        "b_igate": nrm(ks[12], (DEPTH, WIDTH_B), 0.01),
        "lru_lambda": jnp.log(a_base) - jnp.log1p(-a_base),
        "w_out": nrm(ks[13], (DEPTH, MIX_WIDTH, D_MODEL), MIX_WIDTH ** -0.5),
        "norm_x_g": 1.0 + nrm(ks[14], (DEPTH, D_MODEL), 0.02),
        "norm_mem_g": 1.0 + nrm(ks[15], (DEPTH, D_MODEL), 0.02),
        "w_q": nrm(ks[16], (DEPTH, D_MODEL, D_MODEL), D_MODEL ** -0.5),
        "w_kv": nrm(ks[17], (DEPTH, D_MODEL, 2 * D_MODEL), D_MODEL ** -0.5),
        "w_o": nrm(ks[18], (DEPTH, D_MODEL, D_MODEL), D_MODEL ** -0.5),
        "norm_f_g": 1.0 + nrm(ks[19], (D_MODEL,), 0.02),
    }

def reference(x, mem, norm_mix_g, w_in, conv_a_w, conv_a_b, conv_b_w, conv_b_b,
              w_rgate, b_rgate, w_igate, b_igate, lru_lambda, w_out,
              norm_x_g, norm_mem_g, w_q, w_kv, w_o, norm_f_g):
    h = x
    for l in range(DEPTH):
        hn = rms_norm(h, norm_mix_g[l])
        proj = hn @ w_in[l]
        v_a, b_a, c_a, g_a, x_b, g_b = jnp.split(
            proj, np.cumsum([WIDTH_A] * 4 + [WIDTH_B])[:].tolist(), axis=-1)
        y_a = b_a * causal_depthwise_conv(c_a * v_a, conv_a_w[l], conv_a_b[l])
        y_a = y_a * jax.nn.silu(g_a)
        x_c = causal_depthwise_conv(x_b, conv_b_w[l], conv_b_b[l])
        y_b = rg_lru(x_c, w_rgate[l], b_rgate[l], w_igate[l], b_igate[l], lru_lambda[l])
        y_b = y_b * jax.nn.silu(g_b)
        h = h + jnp.concatenate([y_a, y_b], axis=-1) @ w_out[l]
        h = h + memory_cross_attention(rms_norm(h, norm_x_g[l]), rms_norm(mem, norm_mem_g[l]),
                                       w_q[l], w_kv[l], w_o[l])
    return rms_norm(h, norm_f_g)


_drawn_inputs = setup_inputs


def setup_inputs(seed=0):
    import zlib

    import numpy as np

    out = dict(_drawn_inputs(seed))
    spreads = {}
    factors = {'norm_mix_g': 3.364,
     'conv_a_b': 43.589,
     'conv_b_b': 57.664,
     'b_rgate': 64.0,
     'b_igate': 64.0,
     'norm_x_g': 28.575,
     'norm_mem_g': 27.149,
     'norm_f_g': 8.526}
    for name, (base, spread) in spreads.items():
        noise = np.random.default_rng([zlib.crc32(name.encode()), seed]).standard_normal(out[name].shape)
        drawn = base * np.exp(spread * noise) if base else spread * noise
        out[name] = __import__('jax').numpy.asarray(drawn.astype(out[name].dtype))
    for name, factor in factors.items():
        out[name] = (out[name] * factor).astype(out[name].dtype)
    return out
```

```python
from contextlib import ExitStack

import numpy as np

import concourse.bass as bass
from concourse import mybir
from concourse.alu_op_type import AluOpType as ALU

F32 = mybir.dt.float32
F32R = mybir.dt.float32r
ACT = mybir.ActivationFunctionType
AX_X = mybir.AxisListType.X

P = 128
EPS = 1e-6
LRU_C = 8.0
HEADS = 4


def hybrid_layer(nc, x, mem, norm_mix_g, w_in, conv_a_w, conv_a_b, conv_b_w, conv_b_b,
                 w_rgate, b_rgate, w_igate, b_igate, lru_lambda, w_out,
                 norm_x_g, norm_mem_g, w_q, w_kv, w_o, norm_f_g, out):
    S, D = x.shape[1], x.shape[2]
    M = mem.shape[1]
    assert x.shape[0] == 1 and M == S and S == 2 * P
    TT = S // P
    KD = D // P
    KM = w_out.shape[1] // P
    UW = 1024
    PW = 256
    PK = UW // PW
    PU = KD // PK
    MW = 512
    MK = UW // MW
    MT = PW // P
    RING = 4
    HD = D // HEADS
    HC = HD // P
    SCORE_SCALE = float(HD) ** -0.5
    PAIRS = D // PW
    NG = D // MW
    KINDS = (4, 5, 0, 2, 1, 3)
    U_PAIR = len(KINDS) * PU
    U_OUT = PAIRS * U_PAIR
    U_GO = KM // MK
    U_K0 = U_OUT + NG * U_GO
    U_KH = (HD // PW) * PU
    U_V = KD // MK
    U_HEAD = U_KH + U_V + U_KH
    U_ATT = U_K0 + U_KH
    U_LAST = U_ATT + (HEADS - 1) * U_HEAD
    U_WO = U_LAST + U_KH + U_V
    U_END = U_WO + NG * U_V
    assert all(u % RING == 0 for u in (U_PAIR, U_OUT, U_GO, U_K0, U_KH, U_V, U_ATT, U_LAST, U_WO))

    xs = x[0].rearrange("(t p) d -> p t d", p=P)
    ms = mem[0].rearrange("(t p) d -> p t d", p=P)
    outs = out[0].rearrange("(t p) d -> p t d", p=P)
    rows = lambda w: w[0].rearrange("(k p) n -> p k n", p=P)
    win_r, wout_r, wq_r, wkv_r, wo_r = (rows(w) for w in (w_in, w_out, w_q, w_kv, w_o))

    with ExitStack() as ctx:
        def sb(name, shape, dt=F32, stack=ctx):
            return stack.enter_context(nc.sbuf_tensor(name, shape, dt))

        def sem(name):
            return ctx.enter_context(nc.semaphore(name))

        raw = sb("raw", [P, RING, UW])
        w_hi = sb("w_hi", [P, RING, UW], F32R)
        w_lo = sb("w_lo", [P, RING, UW], F32R)
        xT = sb("xT", [P, KD, 2, S], F32R)
        yT = sb("yT", [P, KM, 2, S], F32R)
        h = sb("h", [P, TT, D])
        memb = sb("memb", [P, TT, D])
        ident = sb("ident", [P, P])
        vrows = sb("vrows", [P, 2, P])
        vec = sb("vec", [P, 2, P])
        small = sb("small", [P, 64])
        start = sb("start", [P, 2])
        hT = yT[:, 0:KD]
        oT = yT[:, KD:2 * KD]

        vflat = vec[:, :, :].rearrange("p a b -> p (a b)")
        VN = {n: KD * k for k, n in enumerate(
            ["mix_g", "x_g", "mem_g", "aw0", "aw1", "aw2", "ab", "bw0", "bw1", "bw2", "bw3", "bb", "br", "bi", "lam"])}
        VN["decay"] = VN["lam"] + KD

        def v_(name, m):
            return vflat[:, VN[name] + m:VN[name] + m + 1] if isinstance(m, int) else vflat[:, bass.ds(m + VN[name], 1)]

        x_ss, x_rt, x_rs = small[:, 0:2], small[:, 2:4], small[:, 4:6]
        m_ss, m_rt, m_rs = small[:, 6:8], small[:, 8:10], small[:, 10:12]
        h_ss, h_s1, h_rt, h_rs, h_sc = (small[:, 12:20].rearrange("p (t n) -> p t n", t=2), small[:, 20:22],
                                        small[:, 22:24], small[:, 24:26], small[:, 26:28])
        f_ss, f_s1, f_rt, f_rs = (small[:, 28:36].rearrange("p (t n) -> p t n", t=2), small[:, 36:38],
                                  small[:, 38:40], small[:, 40:42])
        s_max, s_nmax, s_sum, s_rsum = small[:, 42:44], small[:, 44:46], small[:, 46:48], small[:, 48:50]

        acc = ctx.enter_context(nc.psum_tensor("acc", [P, 2, 2, 512], F32))
        aux = ctx.enter_context(nc.psum_tensor("aux", [P, 4, 512], F32))

        raw_landed = [sem(f"raw_landed{s}") for s in range(RING)]
        raw_freed = sem("raw_freed")
        wait_carrier = sem("wait_carrier")
        hi_ready = sem("hi_ready")
        units_used = sem("units_used")
        acc_freed = sem("acc_freed")
        ident_zero, ident_ready = sem("ident_zero"), sem("ident_ready")
        vrows_landed, vec_turned, vec_ready = sem("vrows_landed"), sem("vec_turned"), sem("vec_ready")
        softplus_act, softplus_step, softplus_dve = sem("softplus_act"), sem("softplus_step"), sem("softplus_dve")
        x_landed = [sem(f"x_landed{t}") for t in range(TT)]
        x_stat, x_scaled = sem("x_stat"), sem("x_scaled")
        turn_done, turn_hi, turn_lo = sem("turn_done"), sem("turn_hi"), sem("turn_lo")
        pads_zero = sem("pads_zero")
        half_ready = sem("half_ready")
        gate_w_landed, gates_done = sem("gate_w_landed"), sem("gates_done")
        conv_b_step, gb_sig = sem("conv_b_step"), sem("gb_sig")
        gate_sig, tanh_ready = sem("gate_sig"), sem("tanh_ready")
        d1_ready, d_ready, s_ready, q_ready, a_ready = (sem("one_plus_t"), sem("d_ready"), sem("s_ready"),
                                                       sem("q_ready"), sem("a_ready"))
        mult_ready, mult_first, ixc_ready, u_ready = sem("mult_ready"), sem("mult_first"), sem("ixc_ready"), sem("u_ready")
        scanned, gb_silu, yb_ready, yb_hi, yb_lo = sem("scanned"), sem("gb_silu"), sem("yb_ready"), sem("yb_hi"), sem("yb_lo")
        cv_ready, conv_a_step, ba_conv, ga_sig = sem("cv_ready"), sem("conv_a_step"), sem("ba_conv"), sem("ga_sig")
        ga_silu, ya_ready, ya_hi, ya_lo = sem("ga_silu"), sem("ya_ready"), sem("ya_hi"), sem("ya_lo")
        mem_landed, mem_stat, mem_staged = sem("mem_landed"), sem("mem_stat"), sem("mem_staged")
        h_squared, h_stat = sem("h_squared"), sem("h_stat")
        scores_done, score_max, exp_done, exp_scale = sem("scores_done"), sem("score_max"), sem("exp_done"), sem("exp_scale")
        p_turned, pt_ready, v_act = sem("p_turned"), sem("pt_ready"), sem("v_act")
        pv_done, o_hi, o_lo = sem("pv_done"), sem("o_hi"), sem("o_lo")
        fg_landed, o_squared, f_stat = sem("fg_landed"), sem("o_squared"), sem("f_stat")
        f_ready, stored = sem("f_ready"), sem("stored")

        with ExitStack() as first:
            xn = sb("xn", [P, TT, D], stack=first)
            sp = sb("sp", [P, 8, KD], stack=first)
            junk = sb("junk", [P, 2, D // 2], stack=first)
        with ExitStack() as mixer:
            def tile(name, pad=0):
                return sb(name, [P, MT, S + pad], stack=mixer)
            half = tile("half")
            xb = tile("xb", 3)
            cv = tile("cv", 2)
            xc, g_pre, g_sig = tile("xc"), tile("g_pre"), tile("g_sig")
            t2, ig, dd, ss, qq, aa, va = (tile(n) for n in ("t2", "ig", "dd", "ss", "qq", "aa", "va"))
            gw = sb("gw", [P, 2, MT, P], stack=mixer)
            ba, ca, conv_a = t2, dd, ss
        with ExitStack() as later:
            stage = sb("stage", [P, TT, MW], stack=later)
            junk_a = sb("junk_a", [P, D], stack=later)
            junk_v = sb("junk_v", [P, D], stack=later)
        attention = ctx
        half_k = sb("half_k", [P, MT, S], stack=attention)
        kT = sb("kT", [P, HC, M], stack=attention)
        qT = sb("qT", [P, HC, S], stack=attention)
        vv = sb("vv", [P, TT, HD], stack=attention)
        pp = sb("pp", [P, TT, M], stack=attention)
        pT = sb("pT", [P, TT, S], stack=attention)
        fg = sb("fg", [P, D], stack=attention)

        block = ctx.enter_context(nc.Block())

        @block.sync
        def _(sp_):
            for t in range(TT):
                for c in range(2):
                    sp_.dma_start(h[:, t, c * (D // 2):(c + 1) * (D // 2)],
                                  xs[:, t, c * (D // 2):(c + 1) * (D // 2)]).then_inc(x_landed[t], 16)

            def unit(i, per, c, w, k0, nk, base, col, width):
                first_column = base + col
                if not isinstance(base, int):
                    first_column = sp_.snap(first_column)
                sp_.wait_ge(raw_freed, i * per + c + 1)
                if not isinstance(base, int) and k0 == col == 0:
                    sp_.sem_inc(wait_carrier, 1)
                dst = raw[:, c % RING, :].rearrange("p (k n) -> p k n", k=nk)
                src = w[:, k0:k0 + nk, bass.ds(first_column, width)]
                sp_.dma_start(dst, src).then_inc(raw_landed[c % RING], 16)

            with sp_.Fori(0, PAIRS) as i:
                for g, kind in enumerate(KINDS):
                    for q in range(PU):
                        unit(i, U_PAIR, g * PU + q, win_r, q * PK, PK, i * PW, kind * D, PW)
            with sp_.Fori(0, NG // 2) as i:
                for s in range(2):
                    for q in range(U_GO):
                        unit(i, 2 * U_GO, U_OUT + s * U_GO + q, wout_r, q * MK, MK, i * (2 * MW), s * MW, MW)

            def keys(i, per, u, base, col, w):
                for g in range(HD // PW):
                    for q in range(PU):
                        unit(i, per, u + g * PU + q, w, q * PK, PK, base, col + g * PW, PW)

            def values(i, per, u, base, col, w):
                for q in range(U_V):
                    unit(i, per, u + q, w, q * MK, MK, base, col, MW)

            keys(0, 0, U_K0, 0, 0, wkv_r)
            with sp_.Fori(0, HEADS - 1) as i:
                keys(i, U_HEAD, U_ATT, i * HD, 0, wq_r)
                values(i, U_HEAD, U_ATT + U_KH, i * HD, D, wkv_r)
                keys(i, U_HEAD, U_ATT + U_KH + U_V, i * HD, HD, wkv_r)
            keys(0, 0, U_LAST, 0, (HEADS - 1) * HD, wq_r)
            values(0, 0, U_LAST + U_KH, 0, D + (HEADS - 1) * HD, wkv_r)
            for n in range(NG):
                values(0, 0, U_WO + n * U_V, 0, n * MW, wo_r)

            for k in range(2 * TT):
                t, c = k // 2, k % 2
                sp_.wait_ge(f_ready, k + 1)
                cols = slice(c * (D // 2), (c + 1) * (D // 2))
                sp_.dma_start(outs[:, t, cols], h[:, t, cols]).then_inc(stored, 16)
            sp_.wait_ge(stored, 16 * 2 * TT)

        @block.gpsimd
        def _(pool):
            at = 0
            for src in (norm_mix_g, norm_x_g, norm_mem_g, conv_a_w[0], conv_a_b, conv_b_w[0], conv_b_b,
                        b_rgate, b_igate, lru_lambda):
                r = src.rearrange("k (m c) -> (k m) c", c=P)
                n = r.shape[0]
                done = 0
                while done < n:
                    k = min(n - done, P - at % P)
                    pool.dma_start(vrows[at % P:at % P + k, at // P, :], r[done:done + k, :]).then_inc(vrows_landed, 16)
                    at, done = at + k, done + k
            pool.memset(ident[:], 0.0).then_inc(ident_zero, 1)
            pool.wait_ge(ident_zero, 1)
            pool.affine_select(out=ident[:], in_=ident[:], compare_op=ALU.not_equal, fill=1.0, base=0,
                               pattern=[[-1, P]], channel_multiplier=1).then_inc(ident_ready, 1)

            def gate_weights(head):
                heads = slice(head, head + MT) if isinstance(head, int) else bass.ds(head, MT)
                for k, w in enumerate((w_rgate, w_igate)):
                    pool.dma_start(gw[:, k], w[0, heads].rearrange("m i j -> i m j")).then_inc(gate_w_landed, 16)

            gate_weights(0)
            pool.wait_ge(units_used, PU)
            pool.dma_start(memb[:], ms).then_inc(mem_landed, 16)
            with pool.Fori(1, PAIRS) as i:
                pool.wait_ge(gates_done, i)
                gate_weights(i * MT)
            pool.wait_ge(turn_lo, 3 * KD)
            pool.dma_start(fg[:], norm_f_g.rearrange("(o d) -> o d", o=1).to_broadcast([P, D])).then_inc(fg_landed, 16)

        @block.tensor
        def _(pe):
            def project_unit(i, per, c, src, a, q):
                s = c % RING
                pe.wait_ge(raw_freed, i * per + c + 1 + RING)
                for kk in range(PK):
                    kc = q * PK + kk
                    for m in range(MT):
                        wh = w_hi[:, s, kk * PW + m * P:kk * PW + (m + 1) * P]
                        wl = w_lo[:, s, kk * PW + m * P:kk * PW + (m + 1) * P]
                        both = (acc[:, a, m, :], wh, src[:, kc].rearrange("p a b -> p (a b)"))
                        high = (acc[:, a, m, 0:S], wl, src[:, kc, 0, :])
                        last = kc == KD - 1
                        for o, l, r in ((high, both) if last else (both, high)):
                            mm = nc.tensor.matmul(o, l, r, start=kc == 0 and l is wh, stop=last and l is wh)
                mm.then_inc(units_used, 1)

            def mix_unit(i, per, c, src, a, q, nk):
                s = c % RING
                pe.wait_ge(raw_freed, i * per + c + 1 + RING)
                for kk in range(MK):
                    kc = q * MK + kk
                    wh, wl = (w[:, s, kk * MW:(kk + 1) * MW] for w in (w_hi, w_lo))
                    for t in range(TT):
                        o = acc[:, a, t, :]
                        hi, lo = (src[:, kc, k, t * P:(t + 1) * P] for k in range(2))
                        nc.tensor.matmul(o, hi, wh, start=kc == 0, stop=False)
                        nc.tensor.matmul(o, hi, wl, start=False, stop=False)
                        mm = nc.tensor.matmul(o, lo, wh, start=False, stop=kc == nk - 1)
                mm.then_inc(units_used, 1)

            def turn(src, c):
                for t in range(TT):
                    mm = nc.tensor.transpose(aux[:, c % 4, t * P:(t + 1) * P], src[:, t, c * P:(c + 1) * P], ident[:])
                mm.then_inc(turn_done, 1)

            pe.wait_ge(ident_ready, 1)
            pe.wait_ge(vrows_landed, 16 * 11)
            for k in range(2):
                rows_k = P if k == 0 else (15 * KD - P)
                mm = nc.tensor.transpose(aux[:, 0, k * P:k * P + rows_k], vrows[0:rows_k, k, :], ident[0:rows_k, 0:rows_k])
            mm.then_inc(vec_turned, 1)
            pe.wait_ge(vec_ready, 1)
            pe.wait_ge(x_scaled, 2)
            for c in range(KD):
                if c >= 4:
                    pe.wait_ge(turn_lo, c - 3)
                turn(xn, c)
            pe.wait_ge(turn_lo, KD)

            with pe.Fori(0, PAIRS) as i:
                for g in range(len(KINDS)):
                    pe.wait_ge(acc_freed, i * len(KINDS) + g + 1)
                    for q in range(PU):
                        c = g * PU + q
                        project_unit(i, U_PAIR, c, xT, g % 2, q)
                        if c == 6:
                            pe.wait_ge(gate_w_landed, i * 32 + 32)
                            pe.wait_ge(conv_b_step, i * 8 + 8)
                            for k in range(2):
                                for m in range(MT):
                                    mm = nc.tensor.matmul(aux[:, k, m * S:(m + 1) * S], gw[:, k, m, :], xc[:, m, :],
                                                          start=True, stop=True)
                            mm.then_inc(gates_done, 1)
            G0 = PAIRS * len(KINDS)

            with pe.Fori(0, NG // 2) as i:
                for s in range(2):
                    pe.wait_ge(acc_freed, i * 2 + G0 + s + 1)
                    for q in range(U_GO):
                        if s == 0 and q == 0:
                            pe.wait_ge(ya_lo, PAIRS)
                            pe.wait_ge(yb_lo, PAIRS)
                        mix_unit(i, 2 * U_GO, U_OUT + s * U_GO + q, yT, s, q, KM)
                        if 4 <= q < 8:
                            if q == 4:
                                pe.wait_ge(mem_staged, i * 4 + 2 * s + 2)
                            pe.wait_ge(turn_lo, i * 8 + KD + 4 * s + (q - 4) - 3)
                            for t in range(TT):
                                mm = nc.tensor.transpose(aux[:, q - 4, t * P:(t + 1) * P],
                                                         stage[:, t, (q - 4) * P:(q - 3) * P], ident[:])
                            mm.then_inc(turn_done, 1)
            G0 += NG

            pe.wait_ge(turn_lo, 2 * KD)
            for g in range(2):
                pe.wait_ge(acc_freed, G0 + g + 1)
                for q in range(PU):
                    project_unit(0, 0, U_K0 + g * PU + q, xT, g, q)
                    for c in (2 * (g * PU + q), 2 * (g * PU + q) + 1):
                        if c % 4 == 0:
                            pe.wait_ge(acc_freed, G0 - NG + c // 4 + 3)
                        pe.wait_ge(turn_lo, 2 * KD + c - 3)
                        turn(h, c)
            G0 += 2

            def scores(groups):
                pe.wait_ge(acc_freed, groups + 4)
                for t in range(TT):
                    for d in range(HC):
                        mm = nc.tensor.matmul(aux[:, 0, t * M:(t + 1) * M], qT[:, d, t * P:(t + 1) * P], kT[:, d, :],
                                              start=d == 0, stop=d == HC - 1)
                mm.then_inc(scores_done, 1)

            def turn_p(i):
                pe.wait_ge(exp_scale, i * 3 + 3)
                for mk in range(TT):
                    for t in range(TT):
                        mm = nc.tensor.transpose(aux[:, 1, mk * S + t * P:mk * S + (t + 1) * P],
                                                 pp[:, t, mk * P:(mk + 1) * P], ident[:])
                mm.then_inc(p_turned, 1)

            def weigh_values(i, groups):
                pe.wait_ge(pt_ready, i + 1)
                pe.wait_ge(acc_freed, groups + 5)
                for d in range(HC):
                    for mk in range(TT):
                        mm = nc.tensor.matmul(aux[:, 2 + d // 2, (d % 2) * S:(d % 2 + 1) * S],
                                              vv[:, mk, d * P:(d + 1) * P], pT[:, mk, :], start=mk == 0, stop=mk == TT - 1)
                mm.then_inc(pv_done, 1)

            def queries_values(i, per, u, groups, head):
                pe.wait_ge(acc_freed, groups + 2)
                for g in range(2):
                    for q in range(PU):
                        project_unit(i, per, u + g * PU + q, hT, g, q)
                pe.wait_ge(acc_freed, groups + 3)
                for q in range(U_V):
                    mix_unit(i, per, u + U_KH + q, xT, 0, q, KD)
                    if q == 1:
                        scores(groups)
                    if q == 5:
                        turn_p(head)

            pe.wait_ge(turn_lo, 3 * KD)
            with pe.Fori(0, HEADS - 1) as i:
                queries_values(i, U_HEAD, U_ATT, i * 5 + G0, i)
                for g in range(2):
                    a = 1 - g
                    pe.wait_ge(acc_freed, i * 5 + G0 + 3 + g + 1)
                    for q in range(PU):
                        project_unit(i, U_HEAD, U_ATT + U_KH + U_V + g * PU + q, xT, a, q)
                weigh_values(i, i * 5 + G0)
            G0 += 5 * (HEADS - 1)
            queries_values(0, 0, U_LAST, G0, HEADS - 1)
            G0 += 3
            for n in range(NG):
                pe.wait_ge(acc_freed, G0 + n + 1)
                for q in range(U_V):
                    if n == 0:
                        pe.wait_ge(o_lo, 2 * ((q * MK) // HC + 1))
                    mix_unit(0, 0, U_WO + n * U_V + q, oT, (n + 1) % 2, q, KD)
                    if n == 0 and q == 1:
                        weigh_values(HEADS - 1, G0 - 3)

        @block.scalar
        def _(act):
            def high(i, per, c):
                s = c % RING
                act.wait_ge(raw_landed[s], i * (per // RING * 16) + (c // RING + 1) * 16)
                if c >= RING:
                    act.wait_ge(units_used, i * per + c + 1 - RING)
                nc.scalar.activation(w_hi[:, s, :], raw[:, s, :], ACT.Copy).then_inc(hi_ready, 1)

            act.wait_ge(x_landed[0], 32)
            nc.scalar.activation(junk[:].rearrange("p a b -> p (a b)"), h[:, 0, :], ACT.Square,
                                 accum_out=x_ss[:, 0:1]).then_inc(x_stat, 1)
            act.wait_ge(x_stat, 3)
            nc.scalar.activation(x_rt, x_rs, ACT.Sqrt).then_inc(x_stat, 1)
            act.wait_ge(x_stat, 5)
            nc.scalar.activation(xn[:, 0, :], h[:, 0, :], ACT.Copy, scale=x_rs[:, 0:1]).then_inc(x_scaled, 1)
            act.wait_ge(vec_ready, 1)
            high(0, 0, 0)
            high(0, 0, 1)

            def turned_high(dst, gain, count, bank):
                act.wait_ge(turn_done, count)
                nc.scalar.activation(dst, aux[:, bank, 0:S], ACT.Copy, scale=gain).then_inc(turn_hi, 1)

            for c in range(KD):
                turned_high(xT[:, c, 0, :], v_("mix_g", c), c + 1, c % 4)
            high(0, 0, 2)
            high(0, 0, 3)
            lam = vflat[:, VN["lam"]:VN["lam"] + KD]
            nc.scalar.activation(sp[:, 0, :], lam, ACT.Abs).then_inc(softplus_act, 1)
            act.wait_ge(softplus_act, 1)
            nc.scalar.activation(sp[:, 1, :], sp[:, 0, :], ACT.Exp, scale=-1.0).then_inc(softplus_act, 1)

            def copy_half(dst, a, freed):
                act.wait_ge(acc_freed, freed)
                nc.scalar.activation(dst[:], acc[:, a, :, S:2 * S], ACT.Copy).then_inc(half_ready, 1)

            act.wait_ge(softplus_dve, 1)
            with act.Fori(0, PAIRS) as i:
                for c in range(U_PAIR):
                    high(i, U_PAIR, c + RING)
                    g = c // PU
                    if c % PU == PU - 1:
                        copy_half(half, g % 2, i * len(KINDS) + 2 + g)
                    if c == 7:
                        act.wait_ge(gates_done, i + 1)
                        for m in range(MT):
                            nc.scalar.activation(t2[:, m, :], aux[:, 0, m * S:(m + 1) * S], ACT.Sigmoid,
                                                 bias=v_("br", i * MT + m)).then_inc(gate_sig, 1)
                            nc.scalar.activation(ig[:, m, :], aux[:, 1, m * S:(m + 1) * S], ACT.Sigmoid,
                                                 bias=v_("bi", i * MT + m)).then_inc(gate_sig, 1)
                        act.wait_ge(gate_sig, i * 4 + 4)
                        for m in range(MT):
                            nc.scalar.activation(t2[:, m, :], t2[:, m, :], ACT.Tanh,
                                                 scale=v_("decay", i * MT + m)).then_inc(tanh_ready, 1)
                    if c == 8:
                        act.wait_ge(acc_freed, i * len(KINDS) + 4)
                        nc.scalar.activation(g_sig[:], g_pre[:], ACT.Sigmoid).then_inc(gb_sig, 1)
                    if c == 11:
                        act.wait_ge(q_ready, i + 1)
                        nc.scalar.activation(qq[:], qq[:], ACT.Sqrt, scale=-4.0).then_inc(mult_ready, 1)
                    if c == 14:
                        act.wait_ge(yb_ready, i + 1)
                        nc.scalar.activation(yT[:, bass.ds(i * MT + KD, MT), 0, :], qq[:], ACT.Copy).then_inc(yb_hi, 1)
                    if c == 23:
                        act.wait_ge(acc_freed, i * len(KINDS) + 8)
                        nc.scalar.activation(g_sig[:], g_pre[:], ACT.Sigmoid).then_inc(ga_sig, 1)
                        act.wait_ge(ya_ready, i + 1)
                        nc.scalar.activation(yT[:, bass.ds(i * MT, MT), 0, :], va[:], ACT.Copy).then_inc(ya_hi, 1)
            HALVES = PAIRS * len(KINDS)

            act.wait_ge(ya_lo, PAIRS)
            act.wait_ge(mem_landed, 16)
            nc.scalar.activation(junk_a[:], memb[:, 0, :], ACT.Square, accum_out=m_ss[:, 0:1]).then_inc(mem_stat, 1)
            act.wait_ge(mem_stat, 3)
            nc.scalar.activation(m_rt, m_rs, ACT.Sqrt).then_inc(mem_stat, 1)

            with act.Fori(0, NG // 2) as i:
                for s in range(2):
                    for q in range(U_GO):
                        c = U_OUT + s * U_GO + q
                        high(i, 2 * U_GO, c + RING)
                        if 5 <= q < 9:
                            k = q - 5
                            turned_high(xT[:, bass.ds(i * 8 + 4 * s + k, 1), 0, :].rearrange("p a b -> p (a b)"),
                                        v_("mem_g", i * 8 + 4 * s + k), i * 8 + KD + 4 * s + k + 1, k)
                        if q == U_GO - 1:
                            act.wait_ge(acc_freed, i * 2 + HALVES + s + 3)
                            for t in range(TT):
                                nc.scalar.activation(junk_a[:, 0:MW], h[:, t, bass.ds(i * (2 * MW) + s * MW, MW)], ACT.Square,
                                                     accum_out=h_ss[:, t, bass.ds(i * 2 + s, 1)]).then_inc(h_squared, 1)
                                act.wait_ge(h_squared, i * 4 + 2 * s + t + 1)
            GH = 0
            for c in range(U_KH):
                high(0, 0, U_K0 + c + RING)
                for k in (2 * c, 2 * c + 1):
                    turned_high(hT[:, k, 0, :], v_("x_g", k), 2 * KD + k + 1, k % 4)
                if c == 1:
                    act.wait_ge(h_stat, 2)
                    nc.scalar.activation(h_rt, h_rs, ACT.Sqrt).then_inc(h_stat, 1)
                if c % PU == PU - 1:
                    copy_half(half_k, c // PU, HALVES + NG + 2 + c // PU)

            def softmax(i):
                act.wait_ge(score_max, i * 2 + 2)
                for t in range(TT):
                    nc.scalar.activation(pp[:, t, :], aux[:, 0, t * M:(t + 1) * M], ACT.Exp, bias=s_nmax[:, t:t + 1],
                                         scale=h_sc[:, t:t + 1], accum_out=s_sum[:, t:t + 1]).then_inc(exp_done, 1)

            def queries_values(i, per, u, groups, head):
                for c in range(U_KH + U_V):
                    high(i, per, u + c + RING)
                    if c in (PU - 1, 2 * PU - 1):
                        copy_half(half_k, c // PU, groups + 2 + c // PU)
                    if c == U_KH + 2:
                        softmax(head)
                    if c == U_KH + 6:
                        act.wait_ge(p_turned, head + 1)
                        nc.scalar.activation(pT[:].rearrange("p a b -> p (a b)"), aux[:, 1, :], ACT.Copy).then_inc(pt_ready, 1)
                    if c == U_KH + U_V - 1:
                        nc.scalar.activation(vv[:, 0, :], acc[:, 0, 0, :], ACT.Copy).then_inc(v_act, 1)

            def heads_out(head):
                act.wait_ge(pv_done, head + 1)
                for b in range(2):
                    o = oT[:, bass.ds(head * HC + 2 * b, 2), 0, :] if not isinstance(head, int) else \
                        oT[:, head * HC + 2 * b:head * HC + 2 * b + 2, 0, :]
                    nc.scalar.activation(o, aux[:, 2 + b, :].rearrange("p (a b) -> p a b", a=2), ACT.Copy).then_inc(o_hi, 1)

            G0 = HALVES + NG + 2
            with act.Fori(0, HEADS - 1) as i:
                queries_values(i, U_HEAD, U_ATT, i * 5 + G0, i)
                for c in range(U_KH):
                    high(i, U_HEAD, U_ATT + U_KH + U_V + c + RING)
                    if c in (PU - 1, 2 * PU - 1):
                        g = c // PU
                        copy_half(half_k, 1 - g, i * 5 + G0 + 3 + 2 + g)
                heads_out(i)
            G0 += 5 * (HEADS - 1)
            queries_values(0, 0, U_LAST, G0, HEADS - 1)
            for n in range(NG):
                for q in range(U_V):
                    u = U_WO + n * U_V + q
                    if u + RING < U_END:
                        high(0, 0, u + RING)
                    if n == 0 and q == 1:
                        heads_out(HEADS - 1)
                    if q == U_V - 1:
                        act.wait_ge(acc_freed, G0 + 3 + n + 3)
                        for t in range(TT):
                            if n + t:
                                act.wait_ge(o_squared, n * 2 + t)
                            nc.scalar.activation(pp[:].rearrange("p a b -> p (a b)"), h[:, t, n * MW:(n + 1) * MW], ACT.Square,
                                                 accum_out=f_ss[:, t, n:n + 1]).then_inc(o_squared, 1)
            act.wait_ge(f_stat, 2)
            nc.scalar.activation(f_rt, f_rs, ACT.Sqrt).then_inc(f_stat, 1)

        @block.vector
        def _(dve):
            v = nc.vector

            def low(i, per, c):
                s = c % RING
                dve.wait_ge(hi_ready, i * per + c + 1)
                v.tensor_tensor(w_lo[:, s, :], raw[:, s, :], w_hi[:, s, :].bitcast(F32), ALU.subtract).then_inc(raw_freed, 1)

            v.memset(start[:, 0:1], 0.0).then_inc(raw_freed, RING)
            v.memset(start[:, 1:2], 0.0).then_inc(acc_freed, 2)
            dve.wait_ge(vec_turned, 1)
            v.tensor_copy(vflat[:, 0:15 * KD], aux[:, 0, 0:15 * KD]).then_inc(vec_ready, 1)
            dve.wait_ge(x_landed[1], 32)
            v.tensor_tensor_reduce(xn[:, 1, :], h[:, 1, :], h[:, 1, :], 1.0, 0.0, ALU.mult, ALU.add,
                                   x_ss[:, 1:2]).then_inc(x_stat, 1)
            dve.wait_ge(x_stat, 2)
            v.tensor_scalar(x_rs, x_ss, 1.0 / D, EPS, ALU.mult, ALU.add).then_inc(x_stat, 1)
            dve.wait_ge(x_stat, 4)
            v.reciprocal(x_rs, x_rt).then_inc(x_stat, 1)
            dve.wait_ge(x_stat, 5)
            v.tensor_scalar(xn[:, 1, :], h[:, 1, :], x_rs[:, 1:2], None, ALU.mult).then_inc(x_scaled, 1)
            low(0, 0, 0)
            low(0, 0, 1)

            def turned_low(dst, hi, gain, count, bank):
                dve.wait_ge(turn_hi, count)
                v.scalar_tensor_tensor(out=dst, in0=aux[:, bank, 0:S], scalar=gain, in1=hi.bitcast(F32),
                                       op0=ALU.mult, op1=ALU.subtract).then_inc(turn_lo, 1)

            for c in range(KD):
                turned_low(xT[:, c, 1, :], xT[:, c, 0, :], v_("mix_g", c), c + 1, c % 4)
            low(0, 0, 2)
            low(0, 0, 3)

            steps = [0]

            def chain(ins):
                steps[0] += 1
                ins.then_inc(softplus_step, 1)
                dve.wait_ge(softplus_step, steps[0])

            z, den, r, r2, poly, neg = (sp[:, k, :] for k in range(1, 7))
            lam = vflat[:, VN["lam"]:VN["lam"] + KD]
            dve.wait_ge(softplus_act, 2)
            chain(v.tensor_scalar(den, z, 2.0, None, ALU.add))
            chain(v.reciprocal(r2, den))
            chain(v.tensor_tensor(r, z, r2, ALU.mult))
            chain(v.tensor_tensor(r2, r, r, ALU.mult))
            chain(v.tensor_scalar(poly, r2, 1.0 / 19, None, ALU.mult))
            for k in range(17, 1, -2):
                chain(v.scalar_tensor_tensor(out=poly, in0=poly, scalar=1.0 / k, in1=r2, op0=ALU.add, op1=ALU.mult))
            chain(v.scalar_tensor_tensor(out=poly, in0=poly, scalar=1.0, in1=r, op0=ALU.add, op1=ALU.mult))
            chain(v.tensor_scalar(neg, lam, -1.0, 0.0, ALU.mult, ALU.max))
            chain(v.tensor_scalar(neg, neg, LRU_C / 2, None, ALU.mult))
            v.scalar_tensor_tensor(out=vflat[:, VN["decay"]:VN["decay"] + KD], in0=poly, scalar=LRU_C, in1=neg,
                                   op0=ALU.mult, op1=ALU.add).then_inc(softplus_dve, 1)
            dve.wait_ge(softplus_dve, 1)
            v.memset(xb[:, :, 0:3], 0.0).then_inc(pads_zero, 1)
            v.memset(cv[:, :, 0:2], 0.0).then_inc(pads_zero, 1)
            dve.wait_ge(pads_zero, 2)

            def add_half(dst, a, halves, half_tile, ready=None):
                dve.wait_ge(half_ready, halves)
                v.tensor_tensor(dst, acc[:, a, :, 0:S], half_tile[:], ALU.add).then_inc(acc_freed, 1)

            NK = len(KINDS)
            with dve.Fori(0, PAIRS) as i:
                def freed(g):
                    dve.wait_ge(acc_freed, i * NK + g + 3)

                for c in range(U_PAIR):
                    low(i, U_PAIR, c + RING)
                    if c == 3:
                        add_half(xb[:, :, 3:S + 3], 0, i * NK + 1, half)
                        freed(0)
                    if c in (3, 4):
                        m = c - 3
                        v.tensor_scalar(xc[:, m, :], xb[:, m, 0:S], v_("bw0", i * MT + m), v_("bb", i * MT + m),
                                        ALU.mult, ALU.add).then_inc(conv_b_step, 1)
                        for k in range(1, 4):
                            dve.wait_ge(conv_b_step, i * 8 + 4 * m + k)
                            v.scalar_tensor_tensor(out=xc[:, m, :], in0=xb[:, m, k:k + S], scalar=v_(f"bw{k}", i * MT + m),
                                                   in1=xc[:, m, :], op0=ALU.mult, op1=ALU.add).then_inc(conv_b_step, 1)
                    if c == 7:
                        dve.wait_ge(half_ready, i * NK + 2)
                        v.tensor_tensor(g_pre[:], acc[:, 1, :, 0:S], half[:], ALU.add).then_inc(acc_freed, 1)
                    if c == 8:
                        dve.wait_ge(tanh_ready, i * 2 + 2)
                        v.tensor_scalar(dd[:], t2[:], 1.0, None, ALU.add).then_inc(d1_ready, 1)
                        dve.wait_ge(d1_ready, i + 1)
                        v.reciprocal(dd[:], dd[:]).then_inc(d_ready, 1)
                    if c == 10:
                        dve.wait_ge(d_ready, i + 1)
                        v.tensor_tensor(ss[:], t2[:], dd[:], ALU.mult).then_inc(s_ready, 1)
                        dve.wait_ge(s_ready, i + 1)
                        v.scalar_tensor_tensor(out=qq[:], in0=ss[:], scalar=1.0, in1=ss[:], op0=ALU.subtract,
                                               op1=ALU.mult).then_inc(q_ready, 1)
                        v.tensor_scalar(aa[:], ss[:], -2.0, 1.0, ALU.mult, ALU.add).then_inc(a_ready, 1)
                        v.tensor_tensor(ig[:], ig[:], xc[:], ALU.mult).then_inc(ixc_ready, 1)
                    if c == 11:
                        add_half(va[:], 0, i * NK + 3, half)
                    if c == 12:
                        dve.wait_ge(mult_ready, i + 1)
                        v.memset(qq[:, :, 0:1], 1.0).then_inc(mult_first, 1)
                        dve.wait_ge(mult_first, i + 1)
                        dve.wait_ge(ixc_ready, i + 1)
                        v.tensor_tensor(ig[:], ig[:], qq[:], ALU.mult).then_inc(u_ready, 1)
                        dve.wait_ge(u_ready, i + 1)
                        dve.wait_ge(a_ready, i + 1)
                        for m in range(MT):
                            v.tensor_tensor_scan(dd[:, m, :], aa[:, m, :], ig[:, m, :], 0.0, ALU.mult,
                                                 ALU.add).then_inc(scanned, 1)
                    if c == 13:
                        dve.wait_ge(gb_sig, i + 1)
                        v.tensor_tensor(g_pre[:], g_pre[:], g_sig[:], ALU.mult).then_inc(gb_silu, 1)
                        dve.wait_ge(gb_silu, i + 1)
                        dve.wait_ge(scanned, i * 2 + 2)
                        v.tensor_tensor(qq[:], dd[:], g_pre[:], ALU.mult).then_inc(yb_ready, 1)
                    if c == 14:
                        ky = bass.ds(i * MT + KD, MT)
                        dve.wait_ge(yb_hi, i + 1)
                        v.tensor_tensor(yT[:, ky, 1, :], qq[:], yT[:, ky, 0, :].bitcast(F32), ALU.subtract).then_inc(yb_lo, 1)
                    if c == 15:
                        add_half(ca[:], 1, i * NK + 4, half)
                        freed(3)
                        v.tensor_tensor(cv[:, :, 2:S + 2], ca[:], va[:], ALU.mult).then_inc(cv_ready, 1)
                    if c in (16, 17):
                        m = c - 16
                        dve.wait_ge(cv_ready, i + 1)
                        v.tensor_scalar(conv_a[:, m, :], cv[:, m, 0:S], v_("aw0", i * MT + m), v_("ab", i * MT + m),
                                        ALU.mult, ALU.add).then_inc(conv_a_step, 1)
                        for k in range(1, 3):
                            dve.wait_ge(conv_a_step, i * 6 + 3 * m + k)
                            v.scalar_tensor_tensor(out=conv_a[:, m, :], in0=cv[:, m, k:k + S],
                                                   scalar=v_(f"aw{k}", i * MT + m), in1=conv_a[:, m, :], op0=ALU.mult,
                                                   op1=ALU.add).then_inc(conv_a_step, 1)
                    if c == 19:
                        add_half(ba[:], 0, i * NK + 5, half)
                        freed(4)
                        dve.wait_ge(conv_a_step, i * 6 + 6)
                        v.tensor_tensor(conv_a[:], conv_a[:], ba[:], ALU.mult).then_inc(ba_conv, 1)
                    if c == 23:
                        dve.wait_ge(half_ready, i * NK + 6)
                        v.tensor_tensor(g_pre[:], acc[:, 1, :, 0:S], half[:], ALU.add).then_inc(acc_freed, 1)
                        freed(5)
                        dve.wait_ge(ba_conv, i + 1)
                        v.tensor_tensor(va[:], conv_a[:], g_pre[:], ALU.mult).then_inc(ga_silu, 1)
                        dve.wait_ge(ga_silu, i + 1)
                        dve.wait_ge(ga_sig, i + 1)
                        v.tensor_tensor(va[:], va[:], g_sig[:], ALU.mult).then_inc(ya_ready, 1)
                        ky = bass.ds(i * MT, MT)
                        dve.wait_ge(ya_hi, i + 1)
                        v.tensor_tensor(yT[:, ky, 1, :], va[:], yT[:, ky, 0, :].bitcast(F32), ALU.subtract).then_inc(ya_lo, 1)
            G0 = PAIRS * NK

            dve.wait_ge(ya_lo, PAIRS)
            dve.wait_ge(mem_landed, 16)
            v.tensor_tensor_reduce(junk_v[:], memb[:, 1, :], memb[:, 1, :], 1.0, 0.0, ALU.mult, ALU.add,
                                   m_ss[:, 1:2]).then_inc(mem_stat, 1)
            dve.wait_ge(mem_stat, 2)
            v.tensor_scalar(m_rs, m_ss, 1.0 / D, EPS, ALU.mult, ALU.add).then_inc(mem_stat, 1)
            dve.wait_ge(mem_stat, 4)
            v.reciprocal(m_rs, m_rt).then_inc(mem_stat, 1)
            dve.wait_ge(mem_stat, 5)

            with dve.Fori(0, NG // 2) as i:
                for s in range(2):
                    cols = bass.ds(i * (2 * MW) + s * MW, MW)
                    for q in range(U_GO):
                        c = U_OUT + s * U_GO + q
                        low(i, 2 * U_GO, c + RING)
                        if q == 2:
                            dve.wait_ge(turn_done, i * 8 + KD + 4 * s)
                            for t in range(TT):
                                v.tensor_scalar(stage[:, t, :], memb[:, t, cols], m_rs[:, t:t + 1], None,
                                                ALU.mult).then_inc(mem_staged, 1)
                        if 5 <= q < 9:
                            k = q - 5
                            kc = bass.ds(i * 8 + 4 * s + k, 1)
                            turned_low(xT[:, kc, 1, :].rearrange("p a b -> p (a b)"),
                                       xT[:, kc, 0, :].rearrange("p a b -> p (a b)"),
                                       v_("mem_g", i * 8 + 4 * s + k), i * 8 + KD + 4 * s + k + 1, k)
                        if q == U_GO - 1:
                            dve.wait_ge(units_used, i * (2 * U_GO) + c + 1)
                            v.tensor_tensor(h[:, :, cols], acc[:, s], h[:, :, cols], ALU.add).then_inc(acc_freed, 1)
            G0 += NG

            def stat(total, parts, mean, count_sem, first, wait):
                v.tensor_reduce(total, parts, AX_X, ALU.add).then_inc(count_sem, 1)
                dve.wait_ge(count_sem, first + 1)
                v.tensor_scalar(mean, total, 1.0 / D, EPS, ALU.mult, ALU.add).then_inc(count_sem, 1)

            for c in range(U_KH):
                low(0, 0, U_K0 + c + RING)
                for k in (2 * c, 2 * c + 1):
                    turned_low(hT[:, k, 1, :], hT[:, k, 0, :], v_("x_g", k), 2 * KD + k + 1, k % 4)
                if c == 0:
                    dve.wait_ge(h_squared, 2 * NG)
                    stat(h_s1, h_ss, h_rs, h_stat, 0, None)
                if c == 3:
                    dve.wait_ge(h_stat, 3)
                    v.reciprocal(h_rs, h_rt).then_inc(h_stat, 1)
                    dve.wait_ge(h_stat, 4)
                    v.tensor_scalar(h_sc, h_rs, SCORE_SCALE, None, ALU.mult).then_inc(h_stat, 1)
                    dve.wait_ge(h_stat, 5)
                if c % PU == PU - 1:
                    g = c // PU
                    add_half(kT[:, 2 * g:2 * g + 2, :], g, G0 - NG + g + 1, half_k)
            G0 += 2
            H0 = G0 - NG

            def queries_values(i, per, u, groups, halves, head):
                for c in range(U_KH + U_V):
                    low(i, per, u + c + RING)
                    if c in (PU - 1, 2 * PU - 1):
                        g = c // PU
                        add_half(qT[:, 2 * g:2 * g + 2, :], g, halves + g + 1, half_k)
                    if c == U_KH + 2:
                        dve.wait_ge(scores_done, head + 1)
                        v.tensor_reduce(s_max, aux[:, 0, :].rearrange("p (t m) -> p t m", t=TT), AX_X,
                                        ALU.max).then_inc(score_max, 1)
                        dve.wait_ge(score_max, head * 2 + 1)
                        v.scalar_tensor_tensor(out=s_nmax, in0=s_max, scalar=-1.0, in1=h_sc, op0=ALU.mult,
                                               op1=ALU.mult).then_inc(score_max, 1)
                    if c == U_KH + 3:
                        dve.wait_ge(exp_done, head * 2 + 2)
                        v.reciprocal(s_rsum, s_sum).then_inc(exp_scale, 1)
                        dve.wait_ge(exp_scale, head * 3 + 1)
                        for t in range(TT):
                            v.tensor_scalar(pp[:, t, :], pp[:, t, :], s_rsum[:, t:t + 1], None, ALU.mult).then_inc(exp_scale, 1)
                    if c == U_KH + U_V - 1:
                        dve.wait_ge(v_act, head + 1)
                        v.tensor_copy(vv[:, 1, :], acc[:, 0, 1, :]).then_inc(acc_freed, 1)

            def heads_out(head):
                for b in range(2):
                    kc = slice(head * HC + 2 * b, head * HC + 2 * b + 2) if isinstance(head, int) else bass.ds(head * HC + 2 * b, 2)
                    dve.wait_ge(o_hi, head * 2 + b + 1)
                    v.tensor_tensor(oT[:, kc, 1, :], aux[:, 2 + b, :].rearrange("p (a b) -> p a b", a=2),
                                    oT[:, kc, 0, :].bitcast(F32), ALU.subtract).then_inc(o_lo, 1)

            with dve.Fori(0, HEADS - 1) as i:
                queries_values(i, U_HEAD, U_ATT, i * 5 + G0, i * 4 + H0, i)
                for c in range(U_KH):
                    low(i, U_HEAD, U_ATT + U_KH + U_V + c + RING)
                    if c in (PU - 1, 2 * PU - 1):
                        g = c // PU
                        add_half(kT[:, 2 * g:2 * g + 2, :], 1 - g, i * 4 + H0 + 2 + g + 1, half_k)
                heads_out(i)
            G0 += 5 * (HEADS - 1)
            H0 += 4 * (HEADS - 1)
            queries_values(0, 0, U_LAST, G0, H0, HEADS - 1)
            for n in range(NG):
                for q in range(U_V):
                    u = U_WO + n * U_V + q
                    if u + RING < U_END:
                        low(0, 0, u + RING)
                    if n == 0 and q == 1:
                        heads_out(HEADS - 1)
                    if q == U_V - 1:
                        dve.wait_ge(units_used, u + 1)
                        cols = slice(n * MW, (n + 1) * MW)
                        v.tensor_tensor(h[:, :, cols], acc[:, (n + 1) % 2], h[:, :, cols], ALU.add).then_inc(acc_freed, 1)
            dve.wait_ge(o_squared, 2 * NG)
            stat(f_s1, f_ss, f_rs, f_stat, 0, None)
            dve.wait_ge(f_stat, 3)
            v.reciprocal(f_rs, f_rt).then_inc(f_stat, 1)
            dve.wait_ge(f_stat, 4)
            dve.wait_ge(fg_landed, 16)
            for t in range(TT):
                for c in range(2):
                    cols = slice(c * (D // 2), (c + 1) * (D // 2))
                    v.scalar_tensor_tensor(out=h[:, t, cols], in0=h[:, t, cols], scalar=f_rs[:, t:t + 1], in1=fg[:, cols],
                                           op0=ALU.mult, op1=ALU.mult).then_inc(f_ready, 1)


_INS = ['x', 'mem', 'norm_mix_g', 'w_in', 'conv_a_w', 'conv_a_b', 'conv_b_w', 'conv_b_b', 'w_rgate', 'b_rgate',
        'w_igate', 'b_igate', 'lru_lambda', 'w_out', 'norm_x_g', 'norm_mem_g', 'w_q', 'w_kv', 'w_o', 'norm_f_g']


def kernel(**inputs):
    import concourse.bacc as _bacc
    from concourse.bass_utils import run_bass_kernel_spmd as _run

    nc = _bacc.Bacc("TRN2", target_bir_lowering=False, num_devices=1)
    arrays, args = {}, []
    for name in _INS:
        a = np.ascontiguousarray(inputs[name])
        arrays[f"in_{name}_dram"] = a
        args.append(nc.dram_tensor(f"in_{name}_dram", a.shape, mybir.dt.from_np(a.dtype), kind="ExternalInput").ap())
    shape = np.shape(inputs["x"])
    out = nc.dram_tensor("out_0_dram", shape, F32, kind="ExternalOutput").ap()
    hybrid_layer(nc, *args, out)
    r = _run(nc, [arrays], core_ids=[0])
    return r.results[0]["out_0_dram"]
```

```python
from contextlib import ExitStack

import numpy as np

import concourse.bass as bass
from concourse import mybir
from concourse.alu_op_type import AluOpType as ALU

F32 = mybir.dt.float32
F32R = mybir.dt.float32r
ACT = mybir.ActivationFunctionType
AX_X = mybir.AxisListType.X

P = 128
EPS = 1e-6
LRU_C = 8.0
HEADS = 4


def hybrid_layer(nc, x, mem, norm_mix_g, w_in, conv_a_w, conv_a_b, conv_b_w, conv_b_b,
                 w_rgate, b_rgate, w_igate, b_igate, lru_lambda, w_out,
                 norm_x_g, norm_mem_g, w_q, w_kv, w_o, norm_f_g, out):
    S, D = x.shape[1], x.shape[2]
    M = mem.shape[1]
    assert x.shape[0] == 1 and M == S and S == 2 * P
    TT = S // P
    KD = D // P
    KM = w_out.shape[1] // P
    UW = 1024
    PW = 256
    PK = UW // PW
    PU = KD // PK
    MW = 512
    MK = UW // MW
    MT = PW // P
    RING = 4
    HD = D // HEADS
    HC = HD // P
    SCORE_SCALE = float(HD) ** -0.5
    PAIRS = D // PW
    NG = D // MW
    KINDS = (4, 5, 0, 2, 1, 3)
    U_PAIR = len(KINDS) * PU
    U_OUT = PAIRS * U_PAIR
    U_GO = KM // MK
    U_K0 = U_OUT + NG * U_GO
    U_KH = (HD // PW) * PU
    U_V = KD // MK
    U_HEAD = U_KH + U_V + U_KH
    U_ATT = U_K0 + U_KH
    U_LAST = U_ATT + (HEADS - 1) * U_HEAD
    U_WO = U_LAST + U_KH + U_V
    U_END = U_WO + NG * U_V
    assert all(u % RING == 0 for u in (U_PAIR, U_OUT, U_GO, U_K0, U_KH, U_V, U_ATT, U_LAST, U_WO))

    xs = x[0].rearrange("(t p) d -> p t d", p=P)
    ms = mem[0].rearrange("(t p) d -> p t d", p=P)
    outs = out[0].rearrange("(t p) d -> p t d", p=P)
    rows = lambda w: w[0].rearrange("(k p) n -> p k n", p=P)
    win_r, wout_r, wq_r, wkv_r, wo_r = (rows(w) for w in (w_in, w_out, w_q, w_kv, w_o))

    with ExitStack() as ctx:
        def sb(name, shape, dt=F32, stack=ctx):
            return stack.enter_context(nc.sbuf_tensor(name, shape, dt))

        def sem(name):
            return ctx.enter_context(nc.semaphore(name))

        raw = sb("raw", [P, RING, UW])
        w_hi = sb("w_hi", [P, RING, UW], F32R)
        w_lo = sb("w_lo", [P, RING, UW], F32R)
        xT = sb("xT", [P, KD, 2, S], F32R)
        yT = sb("yT", [P, KM, 2, S], F32R)
        h = sb("h", [P, TT, D])
        memb = sb("memb", [P, TT, D])
        ident = sb("ident", [P, P])
        vrows = sb("vrows", [P, 2, P])
        vec = sb("vec", [P, 2, P])
        small = sb("small", [P, 56 + 2 * PAIRS])
        start = sb("start", [P, 4])
        TURNS_BEFORE = (range(0, 8), range(8, 12), range(12, 16), ())
        UNITS_AMID = (7, 11, 15)
        h_chunks = lambda c: range(min(3 * c, KD), min(3 * c + 3, KD))
        hT = yT[:, 0:KD]
        oT = yT[:, KD:2 * KD]

        vflat = vec[:, :, :].rearrange("p a b -> p (a b)")
        VN = {n: KD * k for k, n in enumerate(
            ["mix_g", "x_g", "mem_g", "aw0", "aw1", "aw2", "ab", "bw0", "bw1", "bw2", "bw3", "bb", "br", "bi", "lam"])}
        VN["decay"] = VN["lam"] + KD

        def v_(name, m):
            return vflat[:, VN[name] + m:VN[name] + m + 1] if isinstance(m, int) else vflat[:, bass.ds(m + VN[name], 1)]

        x_ss, x_ms = small[:, 50:54].rearrange("p (t n) -> p t n", t=2), small[:, 0:2]
        x_rt, x_rs = small[:, 2:4], small[:, 4:6]
        m_ss, m_s1 = small[:, 54:54 + 2 * PAIRS].rearrange("p (t n) -> p t n", t=2), small[:, 6:8]
        m_rt, m_rs = small[:, 8:10], small[:, 10:12]
        h_ss, h_s1, h_rt, h_rs, h_sc = (small[:, 12:20].rearrange("p (t n) -> p t n", t=2), small[:, 20:22],
                                        small[:, 22:24], small[:, 24:26], small[:, 26:28])
        f_ss, f_s1, f_rt, f_rs, f_ms = (small[:, 28:36].rearrange("p (t n) -> p t n", t=2), small[:, 36:38],
                                  small[:, 38:40], small[:, 40:42], small[:, 70:72])
        s_max, s_nmax, s_sum, s_rsum = small[:, 42:44], small[:, 44:46], small[:, 46:48], small[:, 48:50]

        acc = ctx.enter_context(nc.psum_tensor("acc", [P, 2, 2, 512], F32))
        aux = ctx.enter_context(nc.psum_tensor("aux", [P, 4, 512], F32))

        raw_landed = [sem(f"raw_landed{s}") for s in range(RING)]
        raw_freed = sem("raw_freed")
        wait_carrier = sem("wait_carrier")
        hi_ready = sem("hi_ready")
        units_used = sem("units_used")
        acc_freed = sem("acc_freed")
        table_early = sem("table_early")
        ident_zero, ident_ready = sem("ident_zero"), sem("ident_ready")
        vrows_landed, vec_turned, vec_ready = sem("vrows_landed"), sem("vec_turned"), sem("vec_ready")
        softplus_act, softplus_pool, softplus_dve = sem("softplus_act"), sem("softplus_pool"), sem("softplus_dve")
        decay_ready = sem("decay_ready")
        x_landed = [[sem(f"x_landed{t}{c}") for c in range(2)] for t in range(TT)]
        x_stat, x_scaled = sem("x_stat"), [sem(f"x_scaled{t}") for t in range(TT)]
        turn_done, turn_hi, turn_lo = sem("turn_done"), sem("turn_hi"), sem("turn_lo")
        pads_zero = sem("pads_zero")
        half_ready = sem("half_ready")
        gate_w_landed, gates_done = sem("gate_w_landed"), sem("gates_done")
        conv_b_step, gb_sig = sem("conv_b_step"), sem("gb_sig")
        gate_sig, tanh_ready = sem("gate_sig"), sem("tanh_ready")
        d1_ready, d_ready, s_ready, q_ready, a_ready = (sem("one_plus_t"), sem("d_ready"), sem("s_ready"),
                                                       sem("q_ready"), sem("a_ready"))
        mult_ready, mult_first, ixc_ready, u_ready = sem("mult_ready"), sem("mult_first"), sem("ixc_ready"), sem("u_ready")
        scanned, gb_silu, yb_ready, yb_hi, yb_lo = sem("scanned"), sem("gb_silu"), sem("yb_ready"), sem("yb_hi"), sem("yb_lo")
        cv_ready, conv_a_step, ba_conv, ga_sig = sem("cv_ready"), sem("conv_a_step"), sem("ba_conv"), sem("ga_sig")
        ga_silu, ya_ready, ya_hi, ya_lo = sem("ga_silu"), sem("ya_ready"), sem("ya_hi"), sem("ya_lo")
        mem_landed, mem_squared, mem_stat, mem_staged = (sem("mem_landed"), sem("mem_squared"), sem("mem_stat"),
                                                         sem("mem_staged"))
        h_squared, h_stat = sem("h_squared"), sem("h_stat")
        scores_done, score_max, exp_done, exp_scale = sem("scores_done"), sem("score_max"), sem("exp_done"), sem("exp_scale")
        p_turned, pt_ready, v_act = sem("p_turned"), sem("pt_ready"), sem("v_act")
        pv_done, o_hi, o_lo = sem("pv_done"), sem("o_hi"), sem("o_lo")
        fg_landed, o_squared, f_stat = sem("fg_landed"), sem("o_squared"), sem("f_stat")
        first_tile, h_last, gained, out_dve, out_act, stored = (sem("first_tile"), sem("h_last"), sem("gained"),
                                                                sem("out_dve"), sem("out_act"), sem("stored"))

        with ExitStack() as first:
            xn = sb("xn", [P, TT, D], stack=first)
            sp = sb("sp", [P, 8, KD], stack=first)
            junk = sb("junk", [P, 2, D // 2], stack=first)
        with ExitStack() as mixer:
            def tile(name, pad=0):
                return sb(name, [P, MT, S + pad], stack=mixer)
            half = tile("half")
            xb = tile("xb", 3)
            cv = tile("cv", 2)
            xc, g_pre, g_sig = tile("xc"), tile("g_pre"), tile("g_sig")
            t2, ig, dd, ss, qq, aa, va = (tile(n) for n in ("t2", "ig", "dd", "ss", "qq", "aa", "va"))
            gw = sb("gw", [P, 2, MT, P], stack=mixer)
            ba, ca, conv_a = t2, dd, ss
        with ExitStack() as later:
            stage = sb("stage", [P, TT, MW], stack=later)
            junk_a = sb("junk_a", [P, MW], stack=later)
        attention = ctx
        half_k = sb("half_k", [P, MT, S], stack=attention)
        kT = sb("kT", [P, HC, M], stack=attention)
        qT = sb("qT", [P, HC, S], stack=attention)
        vv = sb("vv", [P, TT, HD], stack=attention)
        pp = sb("pp", [P, TT, M], stack=attention)
        pT = sb("pT", [P, TT, S], stack=attention)
        fg = sb("fg", [P, D], stack=attention)
        junk_o = pp[:, :, :].rearrange("p a b -> p (a b)")

        block = ctx.enter_context(nc.Block())

        @block.sync
        def _(sp_):
            for c in range(2):
                for t in range(TT):
                    sp_.dma_start(h[:, t, c * (D // 2):(c + 1) * (D // 2)],
                                  xs[:, t, c * (D // 2):(c + 1) * (D // 2)]).then_inc(x_landed[t][c], 16)

            at = 0
            for src in (norm_mix_g, norm_x_g, norm_mem_g, conv_a_w[0], conv_a_b, conv_b_w[0], conv_b_b,
                        b_rgate, b_igate, lru_lambda):
                r = src.rearrange("k (m c) -> (k m) c", c=P)
                done = 0
                while done < r.shape[0]:
                    k = min(r.shape[0] - done, P - at % P)
                    sp_.dma_start(vrows[at % P:at % P + k, at // P, :], r[done:done + k, :]).then_inc(vrows_landed, 16)
                    at, done = at + k, done + k

            def unit(i, per, c, w, k0, nk, base, col, width):
                first_column = base + col
                if not isinstance(base, int):
                    first_column = sp_.snap(first_column)
                sp_.wait_ge(raw_freed, i * per + c + 1)
                if not isinstance(base, int) and k0 == col == 0:
                    sp_.sem_inc(wait_carrier, 1)
                dst = raw[:, c % RING, :].rearrange("p (k n) -> p k n", k=nk)
                src = w[:, k0:k0 + nk, bass.ds(first_column, width)]
                sp_.dma_start(dst, src).then_inc(raw_landed[c % RING], 16)

            with sp_.Fori(0, PAIRS) as i:
                for g, kind in enumerate(KINDS):
                    for q in range(PU):
                        unit(i, U_PAIR, g * PU + q, win_r, q * PK, PK, i * PW, kind * D, PW)
            with sp_.Fori(0, NG // 2) as i:
                for s in range(2):
                    for q in range(U_GO):
                        unit(i, 2 * U_GO, U_OUT + s * U_GO + q, wout_r, q * MK, MK, i * (2 * MW), s * MW, MW)

            def keys(i, per, u, base, col, w):
                for g in range(HD // PW):
                    for q in range(PU):
                        unit(i, per, u + g * PU + q, w, q * PK, PK, base, col + g * PW, PW)

            def values(i, per, u, base, col, w):
                for q in range(U_V):
                    unit(i, per, u + q, w, q * MK, MK, base, col, MW)

            keys(0, 0, U_K0, 0, 0, wkv_r)
            with sp_.Fori(0, HEADS - 1) as i:
                keys(i, U_HEAD, U_ATT, i * HD, 0, wq_r)
                values(i, U_HEAD, U_ATT + U_KH, i * HD, D, wkv_r)
                keys(i, U_HEAD, U_ATT + U_KH + U_V, i * HD, HD, wkv_r)
            keys(0, 0, U_LAST, 0, (HEADS - 1) * HD, wq_r)
            values(0, 0, U_LAST + U_KH, 0, D + (HEADS - 1) * HD, wkv_r)
            for n in range(NG):
                values(0, 0, U_WO + n * U_V, 0, n * MW, wo_r)

            for t in range(TT):
                for c in range(NG):
                    sp_.wait_ge((out_dve, out_act)[c % 2], t * (NG // 2) + c // 2 + 1)
                    cols = slice(c * MW, (c + 1) * MW)
                    sp_.dma_start(outs[:, t, cols], h[:, t, cols]).then_inc(stored, 16)
            sp_.wait_ge(stored, 16 * TT * NG)

        @block.gpsimd
        def _(pool):
            pool.memset(ident[:], 0.0).then_inc(ident_zero, 1)
            pool.wait_ge(ident_zero, 1)
            pool.affine_select(out=ident[:], in_=ident[:], compare_op=ALU.not_equal, fill=1.0, base=0,
                               pattern=[[-1, P]], channel_multiplier=1).then_inc(ident_ready, 1)

            def chain(ins):
                steps[0] += 1
                ins.then_inc(softplus_pool, 1)
                pool.wait_ge(softplus_pool, steps[0])

            def gate_weights(head):
                heads = slice(head, head + MT) if isinstance(head, int) else bass.ds(head, MT)
                for k, w in enumerate((w_rgate, w_igate)):
                    pool.dma_start(gw[:, k], w[0, heads].rearrange("m i j -> i m j")).then_inc(gate_w_landed, 16)

            gate_weights(0)

            z, den, inv, r, r2, poly, neg = (sp[:, k, :] for k in range(1, 8))
            lam = vflat[:, VN["lam"]:VN["lam"] + KD]
            steps = [0]
            pool.wait_ge(softplus_act, 2)
            chain(nc.gpsimd.tensor_scalar(den, z, 1.0, 2.0, ALU.mult, ALU.add))
            pool.wait_ge(softplus_dve, 1)
            chain(nc.gpsimd.tensor_tensor(r, z, inv, ALU.mult))
            chain(nc.gpsimd.tensor_tensor(r2, r, r, ALU.mult))
            chain(nc.gpsimd.tensor_scalar(poly, r2, 1.0 / 19, 1.0 / 17, ALU.mult, ALU.add))
            for k in range(15, 0, -2):
                chain(nc.gpsimd.tensor_tensor(poly, poly, r2, ALU.mult))
                chain(nc.gpsimd.tensor_scalar(poly, poly, 1.0, 1.0 / k, ALU.mult, ALU.add))
            chain(nc.gpsimd.tensor_tensor(poly, poly, r, ALU.mult))
            chain(nc.gpsimd.tensor_scalar(neg, lam, -1.0, 0.0, ALU.mult, ALU.max))
            chain(nc.gpsimd.tensor_scalar(neg, neg, LRU_C / 2, 0.0, ALU.mult, ALU.add))
            chain(nc.gpsimd.tensor_scalar(poly, poly, LRU_C, 0.0, ALU.mult, ALU.add))
            nc.gpsimd.tensor_tensor(vflat[:, VN["decay"]:VN["decay"] + KD], poly, neg, ALU.add).then_inc(decay_ready, 1)

            pool.wait_ge(units_used, PU)
            pool.dma_start(memb[:], ms).then_inc(mem_landed, 16)
            with pool.Fori(1, PAIRS) as i:
                pool.wait_ge(gates_done, i)
                gate_weights(i * MT)
            pool.wait_ge(turn_lo, 3 * KD)
            pool.dma_start(fg[:], norm_f_g.rearrange("(o d) -> o d", o=1).to_broadcast([P, D])).then_inc(fg_landed, 16)

        @block.tensor
        def _(pe):
            def project_unit(i, per, c, src, a, q):
                s = c % RING
                pe.wait_ge(raw_freed, i * per + c + 1 + RING)
                for kk in range(PK):
                    kc = q * PK + kk
                    for m in range(MT):
                        wh = w_hi[:, s, kk * PW + m * P:kk * PW + (m + 1) * P]
                        wl = w_lo[:, s, kk * PW + m * P:kk * PW + (m + 1) * P]
                        both = (acc[:, a, m, :], wh, src[:, kc].rearrange("p a b -> p (a b)"))
                        high = (acc[:, a, m, 0:S], wl, src[:, kc, 0, :])
                        last = kc == KD - 1
                        for o, l, r in ((high, both) if last else (both, high)):
                            mm = nc.tensor.matmul(o, l, r, start=kc == 0 and l is wh, stop=last and l is wh)
                mm.then_inc(units_used, 1)

            def mix_unit(i, per, c, src, a, q, nk, tiles=range(TT)):
                s = c % RING
                pe.wait_ge(raw_freed, i * per + c + 1 + RING)
                for kk in range(MK):
                    kc = q * MK + kk
                    wh, wl = (w[:, s, kk * MW:(kk + 1) * MW] for w in (w_hi, w_lo))
                    for t in tiles:
                        o = acc[:, a, t, :]
                        hi, lo = (src[:, kc, k, t * P:(t + 1) * P] for k in range(2))
                        nc.tensor.matmul(o, hi, wh, start=kc == 0, stop=False)
                        nc.tensor.matmul(o, hi, wl, start=False, stop=False)
                        mm = nc.tensor.matmul(o, lo, wh, start=False, stop=kc == nk - 1)
                if TT - 1 in tiles:
                    mm.then_inc(units_used, 1)
                return mm

            def turn(src, c):
                for t in range(TT):
                    mm = nc.tensor.transpose(aux[:, c % 4, t * P:(t + 1) * P], src[:, t, c * P:(c + 1) * P], ident[:])
                mm.then_inc(turn_done, 1)

            pe.wait_ge(ident_ready, 1)
            pe.wait_ge(vrows_landed, 16 * 11)
            for k in range(2):
                rows_k = P if k == 0 else (15 * KD - P)
                mm = nc.tensor.transpose(aux[:, 0, k * P:k * P + rows_k], vrows[0:rows_k, k, :], ident[0:rows_k, 0:rows_k])
            mm.then_inc(vec_turned, 1)
            def pair(i, first):
                for g in range(len(KINDS)):
                    pe.wait_ge(acc_freed, i * len(KINDS) + g + 1)
                    for q in range(PU):
                        c = g * PU + q
                        if first and c == 0:
                            pe.wait_ge(vec_ready, 1)
                        for k in (TURNS_BEFORE[c] if first and c < PU else ()):
                            if k % 4 == 0:
                                for t in range(TT):
                                    pe.wait_ge(x_scaled[t], k // 4 + 1)
                            if k >= 4:
                                pe.wait_ge(turn_lo, k - 3)
                            turn(xn, k)
                        if first and c < PU:
                            pe.wait_ge(turn_lo, (c + 1) * PK)
                        project_unit(i, U_PAIR, c, xT, g % 2, q)
                        if c == 7:
                            pe.wait_ge(gate_w_landed, i * 32 + 32)
                            pe.wait_ge(conv_b_step, i * 8 + 8)
                            for k in range(2):
                                for m in range(MT):
                                    mm = nc.tensor.matmul(aux[:, k, m * S:(m + 1) * S], gw[:, k, m, :], xc[:, m, :],
                                                          start=True, stop=True)
                            mm.then_inc(gates_done, 1)

            pair(0, True)
            with pe.Fori(1, PAIRS) as i:
                pair(i, False)
            G0 = PAIRS * len(KINDS)

            with pe.Fori(0, NG // 2) as i:
                for s in range(2):
                    pe.wait_ge(acc_freed, i * 2 + G0 + s + 1)
                    for q in range(U_GO):
                        if s == 0 and q == KD // MK - 1:
                            pe.wait_ge(ya_lo, PAIRS)
                        if s == 0 and q == U_GO - 1:
                            pe.wait_ge(yb_lo, PAIRS)
                        mix_unit(i, 2 * U_GO, U_OUT + s * U_GO + q, yT, s, q, KM)
                        if 4 <= q < 8:
                            if q == 4:
                                pe.wait_ge(mem_staged, i * 4 + 2 * s + 2)
                            pe.wait_ge(turn_lo, i * 8 + KD + 4 * s + (q - 4) - 3)
                            for t in range(TT):
                                mm = nc.tensor.transpose(aux[:, q - 4, t * P:(t + 1) * P],
                                                         stage[:, t, (q - 4) * P:(q - 3) * P], ident[:])
                            mm.then_inc(turn_done, 1)
            G0 += NG

            pe.wait_ge(turn_lo, 2 * KD)
            for g in range(2):
                pe.wait_ge(acc_freed, G0 + g + 1)
                for q in range(PU):
                    project_unit(0, 0, U_K0 + g * PU + q, xT, g, q)
                    for c in h_chunks(g * PU + q):
                        if c % 4 == 0:
                            pe.wait_ge(acc_freed, G0 - NG + c // 4 + 3)
                        pe.wait_ge(turn_lo, 2 * KD + c - 3)
                        turn(h, c)
            G0 += 2

            def scores(groups):
                pe.wait_ge(acc_freed, groups + 4)
                for t in range(TT):
                    for d in range(HC):
                        mm = nc.tensor.matmul(aux[:, 0, t * M:(t + 1) * M], qT[:, d, t * P:(t + 1) * P], kT[:, d, :],
                                              start=d == 0, stop=d == HC - 1)
                mm.then_inc(scores_done, 1)

            def turn_p(i):
                pe.wait_ge(exp_scale, i * 3 + 3)
                for mk in range(TT):
                    for t in range(TT):
                        mm = nc.tensor.transpose(aux[:, 1, mk * S + t * P:mk * S + (t + 1) * P],
                                                 pp[:, t, mk * P:(mk + 1) * P], ident[:])
                mm.then_inc(p_turned, 1)

            def weigh_values(i, groups):
                pe.wait_ge(pt_ready, i + 1)
                pe.wait_ge(acc_freed, groups + 5)
                for d in range(HC):
                    for mk in range(TT):
                        mm = nc.tensor.matmul(aux[:, 2 + d // 2, (d % 2) * S:(d % 2 + 1) * S],
                                              vv[:, mk, d * P:(d + 1) * P], pT[:, mk, :], start=mk == 0, stop=mk == TT - 1)
                mm.then_inc(pv_done, 1)

            def queries_values(i, per, u, groups, head):
                for g in range(2):
                    pe.wait_ge(acc_freed, groups + g + 1)
                    for q in range(PU):
                        project_unit(i, per, u + g * PU + q, hT, g, q)
                pe.wait_ge(acc_freed, groups + 3)
                for q in range(U_V):
                    mix_unit(i, per, u + U_KH + q, xT, 0, q, KD)
                    if q == 1:
                        scores(groups)
                    if q == 5:
                        turn_p(head)

            pe.wait_ge(turn_lo, 3 * KD)
            with pe.Fori(0, HEADS - 1) as i:
                queries_values(i, U_HEAD, U_ATT, i * 5 + G0, i)
                for g in range(2):
                    a = 1 - g
                    pe.wait_ge(acc_freed, i * 5 + G0 + 3 + g + 1)
                    for q in range(PU):
                        project_unit(i, U_HEAD, U_ATT + U_KH + U_V + g * PU + q, xT, a, q)
                weigh_values(i, i * 5 + G0)
                pe.wait_ge(acc_freed, i * 5 + G0 + 7)
            G0 += 5 * (HEADS - 1)
            queries_values(0, 0, U_LAST, G0, HEADS - 1)
            G0 += 3
            for n in range(NG):
                pe.wait_ge(acc_freed, G0 + n + 1)
                for q in range(U_V):
                    if n == NG - 1 and q == U_V - RING:
                        for t in range(TT):
                            for k in range(q, U_V):
                                mm = mix_unit(0, 0, U_WO + n * U_V + k, oT, (n + 1) % 2, k, KD, [t])
                            if t == 0:
                                mm.then_inc(first_tile, 1)
                        break
                    if n == 0:
                        pe.wait_ge(o_lo, 2 * ((q * MK) // HC + 1))
                    mix_unit(0, 0, U_WO + n * U_V + q, oT, (n + 1) % 2, q, KD)
                    if n == 0 and q == 1:
                        weigh_values(HEADS - 1, G0 - 3)

        @block.scalar
        def _(act):
            def high(i, per, c):
                s = c % RING
                act.wait_ge(raw_landed[s], i * (per // RING * 16) + (c // RING + 1) * 16)
                if c >= RING:
                    act.wait_ge(units_used, i * per + c + 1 - RING)
                nc.scalar.activation(w_hi[:, s, :], raw[:, s, :], ACT.Copy).then_inc(hi_ready, 1)

            act.wait_ge(raw_freed, RING)
            nc.scalar.activation(start[:, 2:3], start[:, 0:1], ACT.Sqrt).then_inc(table_early, 1)
            for t in range(TT):
                act.wait_ge(x_landed[t][0], 16)
                nc.scalar.activation(junk[:, t], h[:, t, 0:D // 2], ACT.Square,
                                     accum_out=x_ss[:, t, 0:1]).then_inc(x_stat, 1)
            act.wait_ge(x_stat, 6)
            nc.scalar.activation(x_rt, x_ms, ACT.Sqrt).then_inc(x_stat, 1)
            act.wait_ge(x_stat, 8)
            for c in range(0, D, MW):
                nc.scalar.activation(xn[:, 1, c:c + MW], h[:, 1, c:c + MW], ACT.Copy,
                                     scale=x_rs[:, 1:2]).then_inc(x_scaled[1], 1)
            act.wait_ge(vec_ready, 1)
            high(0, 0, 0)

            def turned_high(dst, gain, count, bank):
                act.wait_ge(turn_done, count)
                nc.scalar.activation(dst, aux[:, bank, 0:S], ACT.Copy, scale=gain).then_inc(turn_hi, 1)

            for c in range(KD):
                turned_high(xT[:, c, 0, :], v_("mix_g", c), c + 1, c % 4)
                if c in UNITS_AMID:
                    high(0, 0, UNITS_AMID.index(c) + 1)
            lam = vflat[:, VN["lam"]:VN["lam"] + KD]
            nc.scalar.activation(sp[:, 0, :], lam, ACT.Abs).then_inc(softplus_act, 1)
            act.wait_ge(softplus_act, 1)
            nc.scalar.activation(sp[:, 1, :], sp[:, 0, :], ACT.Exp, scale=-1.0).then_inc(softplus_act, 1)

            def copy_half(dst, a, freed):
                act.wait_ge(acc_freed, freed)
                nc.scalar.activation(dst[:], acc[:, a, :, S:2 * S], ACT.Copy).then_inc(half_ready, 1)

            with act.Fori(0, PAIRS) as i:
                for c in range(U_PAIR):
                    high(i, U_PAIR, c + RING)
                    g = c // PU
                    if c % PU == PU - 1:
                        copy_half(half, g % 2, i * len(KINDS) + 2 + g)
                    if c == 8:
                        act.wait_ge(gates_done, i + 1)
                        for m in range(MT):
                            nc.scalar.activation(t2[:, m, :], aux[:, 0, m * S:(m + 1) * S], ACT.Sigmoid,
                                                 bias=v_("br", i * MT + m)).then_inc(gate_sig, 1)
                            nc.scalar.activation(ig[:, m, :], aux[:, 1, m * S:(m + 1) * S], ACT.Sigmoid,
                                                 bias=v_("bi", i * MT + m)).then_inc(gate_sig, 1)
                        act.wait_ge(gate_sig, i * 4 + 4)
                        act.wait_ge(decay_ready, 1)
                        for m in range(MT):
                            nc.scalar.activation(t2[:, m, :], t2[:, m, :], ACT.Tanh,
                                                 scale=v_("decay", i * MT + m)).then_inc(tanh_ready, 1)
                    if c == 9:
                        act.wait_ge(acc_freed, i * len(KINDS) + 4)
                        nc.scalar.activation(g_sig[:], g_pre[:], ACT.Sigmoid).then_inc(gb_sig, 1)
                    if c == 12:
                        act.wait_ge(q_ready, i + 1)
                        nc.scalar.activation(qq[:], qq[:], ACT.Sqrt, scale=-4.0).then_inc(mult_ready, 1)
                    if c in (16, 20):
                        t = (c - 16) // 4
                        if c == 16:
                            act.wait_ge(mem_landed, 16)
                        nc.scalar.activation(aux[:, 2 + t, 0:PW], memb[:, t, bass.ds(i * PW, PW)], ACT.Square,
                                             accum_out=m_ss[:, t, bass.ds(i, 1)]).then_inc(mem_squared, 1)
                        act.wait_ge(mem_squared, i * TT + t + 1)
                    if c == 15:
                        act.wait_ge(yb_ready, i + 1)
                        nc.scalar.activation(yT[:, bass.ds(i * MT + KD, MT), 0, :], qq[:], ACT.Copy).then_inc(yb_hi, 1)
                    if c == 23:
                        act.wait_ge(acc_freed, i * len(KINDS) + 8)
                        nc.scalar.activation(g_sig[:], g_pre[:], ACT.Sigmoid).then_inc(ga_sig, 1)
                        act.wait_ge(ya_ready, i + 1)
                        nc.scalar.activation(yT[:, bass.ds(i * MT, MT), 0, :], va[:], ACT.Copy).then_inc(ya_hi, 1)
            HALVES = PAIRS * len(KINDS)

            act.wait_ge(mem_stat, 2)
            nc.scalar.activation(m_rt, m_rs, ACT.Sqrt).then_inc(mem_stat, 1)

            with act.Fori(0, NG // 2) as i:
                for s in range(2):
                    for q in range(U_GO):
                        c = U_OUT + s * U_GO + q
                        high(i, 2 * U_GO, c + RING)
                        if 5 <= q < 9:
                            k = q - 5
                            turned_high(xT[:, bass.ds(i * 8 + 4 * s + k, 1), 0, :].rearrange("p a b -> p (a b)"),
                                        v_("mem_g", i * 8 + 4 * s + k), i * 8 + KD + 4 * s + k + 1, k)
                        if q == U_GO - 1:
                            act.wait_ge(acc_freed, i * 2 + HALVES + s + 3)
                            for t in range(TT):
                                nc.scalar.activation(junk_a[:], h[:, t, bass.ds(i * (2 * MW) + s * MW, MW)], ACT.Square,
                                                     accum_out=h_ss[:, t, bass.ds(i * 2 + s, 1)]).then_inc(h_squared, 1)
                                act.wait_ge(h_squared, i * 4 + 2 * s + t + 1)
            GH = 0
            for c in range(U_KH):
                high(0, 0, U_K0 + c + RING)
                for k in h_chunks(c):
                    turned_high(hT[:, k, 0, :], v_("x_g", k), 2 * KD + k + 1, k % 4)
                if c == 6:
                    act.wait_ge(h_stat, 2)
                    nc.scalar.activation(h_rt, h_rs, ACT.Sqrt).then_inc(h_stat, 1)
                if c % PU == PU - 1:
                    copy_half(half_k, c // PU, HALVES + NG + 2 + c // PU)

            def softmax(i):
                act.wait_ge(score_max, i * 2 + 2)
                for t in range(TT):
                    nc.scalar.activation(pp[:, t, :], aux[:, 0, t * M:(t + 1) * M], ACT.Exp, bias=s_nmax[:, t:t + 1],
                                         scale=h_sc[:, t:t + 1], accum_out=s_sum[:, t:t + 1]).then_inc(exp_done, 1)

            def queries_values(i, per, u, groups, head):
                for c in range(U_KH + U_V):
                    high(i, per, u + c + RING)
                    if c in (PU - 1, 2 * PU - 1):
                        copy_half(half_k, c // PU, groups + 2 + c // PU)
                    if c == U_KH + 2:
                        softmax(head)
                    if c == U_KH + 6:
                        act.wait_ge(p_turned, head + 1)
                        nc.scalar.activation(pT[:].rearrange("p a b -> p (a b)"), aux[:, 1, :], ACT.Copy).then_inc(pt_ready, 1)
                    if c == U_KH + U_V - 1:
                        nc.scalar.activation(vv[:, 0, :], acc[:, 0, 0, :], ACT.Copy).then_inc(v_act, 1)

            def heads_out(head):
                act.wait_ge(pv_done, head + 1)
                for b in range(2):
                    o = oT[:, bass.ds(head * HC + 2 * b, 2), 0, :] if not isinstance(head, int) else \
                        oT[:, head * HC + 2 * b:head * HC + 2 * b + 2, 0, :]
                    nc.scalar.activation(o, aux[:, 2 + b, :].rearrange("p (a b) -> p a b", a=2), ACT.Copy).then_inc(o_hi, 1)

            G0 = HALVES + NG + 2
            with act.Fori(0, HEADS - 1) as i:
                queries_values(i, U_HEAD, U_ATT, i * 5 + G0, i)
                for c in range(U_KH):
                    high(i, U_HEAD, U_ATT + U_KH + U_V + c + RING)
                    if c in (PU - 1, 2 * PU - 1):
                        g = c // PU
                        copy_half(half_k, 1 - g, i * 5 + G0 + 3 + 2 + g)
                heads_out(i)
            G0 += 5 * (HEADS - 1)
            queries_values(0, 0, U_LAST, G0, HEADS - 1)
            for n in range(NG):
                for q in range(U_V):
                    u = U_WO + n * U_V + q
                    if u + RING < U_END:
                        high(0, 0, u + RING)
                    if n == 0 and q == 1:
                        heads_out(HEADS - 1)
                    if q == U_V - 1 and n < NG - 1:
                        act.wait_ge(acc_freed, G0 + 3 + n + 3)
                        for t in range(TT):
                            if n + t:
                                act.wait_ge(o_squared, n * TT + t)
                            nc.scalar.activation(junk_o[:], h[:, t, n * MW:(n + 1) * MW], ACT.Square,
                                                 accum_out=f_ss[:, t, n:n + 1]).then_inc(o_squared, 1)
                        if n == 0:
                            nc.scalar.activation(start[:, 3:4], start[:, 0:1], ACT.Sqrt).then_inc(table_early, 1)
            n = NG - 1
            for t in range(TT):
                act.wait_ge(h_last, t + 1)
                act.wait_ge(o_squared, n * TT + t)
                nc.scalar.activation(junk_o[:], h[:, t, n * MW:(n + 1) * MW], ACT.Square,
                                     accum_out=f_ss[:, t, n:n + 1]).then_inc(o_squared, 1)
                act.wait_ge(f_stat, t * 4 + 2)
                nc.scalar.activation(f_rt[:, t:t + 1], f_ms[:, t:t + 1], ACT.Sqrt).then_inc(f_stat, 1)
                act.wait_ge(f_stat, t * 4 + 4)
                for c in range(1, NG, 2):
                    cols = slice(c * MW, (c + 1) * MW)
                    nc.scalar.activation(h[:, t, cols], memb[:, t, cols], ACT.Copy, scale=f_rs[:, t:t + 1]).then_inc(out_act, 1)

        @block.vector
        def _(dve):
            v = nc.vector

            def low(i, per, c):
                s = c % RING
                dve.wait_ge(hi_ready, i * per + c + 1)
                v.tensor_tensor(w_lo[:, s, :], raw[:, s, :], w_hi[:, s, :].bitcast(F32), ALU.subtract).then_inc(raw_freed, 1)

            v.memset(start[:, 0:1], 0.0).then_inc(raw_freed, RING)
            v.memset(start[:, 1:2], 0.0).then_inc(acc_freed, 2)
            for t in range(TT):
                dve.wait_ge(x_landed[t][1], 16)
                v.tensor_tensor_reduce(xn[:, t, 0:D // 2], h[:, t, D // 2:D], h[:, t, D // 2:D], 1.0, 0.0, ALU.mult,
                                       ALU.add, x_ss[:, t, 1:2]).then_inc(x_stat, 1)
            dve.wait_ge(x_stat, 4)
            v.tensor_tensor(x_ms, x_ss[:, :, 0], x_ss[:, :, 1], ALU.add).then_inc(x_stat, 1)
            dve.wait_ge(x_stat, 5)
            v.tensor_scalar(x_ms, x_ms, 1.0 / D, EPS, ALU.mult, ALU.add).then_inc(x_stat, 1)
            dve.wait_ge(x_stat, 7)
            v.reciprocal(x_rs, x_rt).then_inc(x_stat, 1)
            dve.wait_ge(x_stat, 8)
            for c in range(0, D, MW):
                v.tensor_scalar(xn[:, 0, c:c + MW], h[:, 0, c:c + MW], x_rs[:, 0:1], None, ALU.mult).then_inc(x_scaled[0], 1)
            dve.wait_ge(vec_turned, 1)
            v.tensor_copy(vflat[:, 0:15 * KD], aux[:, 0, 0:15 * KD]).then_inc(vec_ready, 1)
            low(0, 0, 0)

            def turned_low(dst, hi, gain, count, bank):
                dve.wait_ge(turn_hi, count)
                v.scalar_tensor_tensor(out=dst, in0=aux[:, bank, 0:S], scalar=gain, in1=hi.bitcast(F32),
                                       op0=ALU.mult, op1=ALU.subtract).then_inc(turn_lo, 1)

            for c in range(KD):
                turned_low(xT[:, c, 1, :], xT[:, c, 0, :], v_("mix_g", c), c + 1, c % 4)
                if c in UNITS_AMID:
                    low(0, 0, UNITS_AMID.index(c) + 1)
            dve.wait_ge(softplus_pool, 1)
            v.reciprocal(sp[:, 3, :], sp[:, 2, :]).then_inc(softplus_dve, 1)
            v.memset(xb[:, :, 0:3], 0.0).then_inc(pads_zero, 1)
            v.memset(cv[:, :, 0:2], 0.0).then_inc(pads_zero, 1)
            dve.wait_ge(pads_zero, 2)

            def add_half(dst, a, halves, half_tile, ready=None):
                dve.wait_ge(half_ready, halves)
                v.tensor_tensor(dst, acc[:, a, :, 0:S], half_tile[:], ALU.add).then_inc(acc_freed, 1)

            NK = len(KINDS)
            with dve.Fori(0, PAIRS) as i:
                def freed(g):
                    dve.wait_ge(acc_freed, i * NK + g + 3)

                for c in range(U_PAIR):
                    low(i, U_PAIR, c + RING)
                    if c == 3:
                        add_half(xb[:, :, 3:S + 3], 0, i * NK + 1, half)
                        freed(0)
                    if c in (3, 4):
                        for k in range(2 * (c - 3), 2 * (c - 3) + 2):
                            for m in range(MT):
                                if k == 0:
                                    v.tensor_scalar(xc[:, m, :], xb[:, m, 0:S], v_("bw0", i * MT + m),
                                                    v_("bb", i * MT + m), ALU.mult, ALU.add).then_inc(conv_b_step, 1)
                                else:
                                    dve.wait_ge(conv_b_step, i * 8 + MT * (k - 1) + m + 1)
                                    v.scalar_tensor_tensor(out=xc[:, m, :], in0=xb[:, m, k:k + S],
                                                           scalar=v_(f"bw{k}", i * MT + m), in1=xc[:, m, :],
                                                           op0=ALU.mult, op1=ALU.add).then_inc(conv_b_step, 1)
                    if c == 7:
                        dve.wait_ge(half_ready, i * NK + 2)
                        v.tensor_tensor(g_pre[:], acc[:, 1, :, 0:S], half[:], ALU.add).then_inc(acc_freed, 1)
                    if c == 9:
                        dve.wait_ge(tanh_ready, i * 2 + 2)
                        v.tensor_scalar(dd[:], t2[:], 1.0, None, ALU.add).then_inc(d1_ready, 1)
                        dve.wait_ge(d1_ready, i + 1)
                        v.reciprocal(dd[:], dd[:]).then_inc(d_ready, 1)
                    if c == 11:
                        dve.wait_ge(d_ready, i + 1)
                        v.tensor_tensor(ss[:], t2[:], dd[:], ALU.mult).then_inc(s_ready, 1)
                        dve.wait_ge(s_ready, i + 1)
                        v.scalar_tensor_tensor(out=qq[:], in0=ss[:], scalar=1.0, in1=ss[:], op0=ALU.subtract,
                                               op1=ALU.mult).then_inc(q_ready, 1)
                        v.tensor_scalar(aa[:], ss[:], -2.0, 1.0, ALU.mult, ALU.add).then_inc(a_ready, 1)
                        v.tensor_tensor(ig[:], ig[:], xc[:], ALU.mult).then_inc(ixc_ready, 1)
                    if c == 11:
                        add_half(va[:], 0, i * NK + 3, half)
                    if c == 13:
                        dve.wait_ge(mult_ready, i + 1)
                        v.memset(qq[:, :, 0:1], 1.0).then_inc(mult_first, 1)
                        dve.wait_ge(mult_first, i + 1)
                        dve.wait_ge(ixc_ready, i + 1)
                        v.tensor_tensor(ig[:], ig[:], qq[:], ALU.mult).then_inc(u_ready, 1)
                        dve.wait_ge(u_ready, i + 1)
                        dve.wait_ge(a_ready, i + 1)
                        for m in range(MT):
                            v.tensor_tensor_scan(dd[:, m, :], aa[:, m, :], ig[:, m, :], 0.0, ALU.mult,
                                                 ALU.add).then_inc(scanned, 1)
                    if c == 14:
                        dve.wait_ge(gb_sig, i + 1)
                        v.tensor_tensor(g_pre[:], g_pre[:], g_sig[:], ALU.mult).then_inc(gb_silu, 1)
                        dve.wait_ge(gb_silu, i + 1)
                        dve.wait_ge(scanned, i * 2 + 2)
                        v.tensor_tensor(qq[:], dd[:], g_pre[:], ALU.mult).then_inc(yb_ready, 1)
                    if c == 15:
                        ky = bass.ds(i * MT + KD, MT)
                        dve.wait_ge(yb_hi, i + 1)
                        v.tensor_tensor(yT[:, ky, 1, :], qq[:], yT[:, ky, 0, :].bitcast(F32), ALU.subtract).then_inc(yb_lo, 1)
                    if c == 15:
                        add_half(ca[:], 1, i * NK + 4, half)
                        freed(3)
                        v.tensor_tensor(cv[:, :, 2:S + 2], ca[:], va[:], ALU.mult).then_inc(cv_ready, 1)
                    if c in (16, 17, 18):
                        k = c - 16
                        if k == 0:
                            dve.wait_ge(cv_ready, i + 1)
                        for m in range(MT):
                            if k == 0:
                                v.tensor_scalar(conv_a[:, m, :], cv[:, m, 0:S], v_("aw0", i * MT + m),
                                                v_("ab", i * MT + m), ALU.mult, ALU.add).then_inc(conv_a_step, 1)
                            else:
                                dve.wait_ge(conv_a_step, i * 6 + MT * (k - 1) + m + 1)
                                v.scalar_tensor_tensor(out=conv_a[:, m, :], in0=cv[:, m, k:k + S],
                                                       scalar=v_(f"aw{k}", i * MT + m), in1=conv_a[:, m, :],
                                                       op0=ALU.mult, op1=ALU.add).then_inc(conv_a_step, 1)
                    if c == 19:
                        add_half(ba[:], 0, i * NK + 5, half)
                        freed(4)
                        dve.wait_ge(conv_a_step, i * 6 + 6)
                        v.tensor_tensor(conv_a[:], conv_a[:], ba[:], ALU.mult).then_inc(ba_conv, 1)
                    if c == 23:
                        dve.wait_ge(half_ready, i * NK + 6)
                        v.tensor_tensor(g_pre[:], acc[:, 1, :, 0:S], half[:], ALU.add).then_inc(acc_freed, 1)
                        freed(5)
                        dve.wait_ge(ba_conv, i + 1)
                        v.tensor_tensor(va[:], conv_a[:], g_pre[:], ALU.mult).then_inc(ga_silu, 1)
                        dve.wait_ge(ga_silu, i + 1)
                        dve.wait_ge(ga_sig, i + 1)
                        v.tensor_tensor(va[:], va[:], g_sig[:], ALU.mult).then_inc(ya_ready, 1)
                        ky = bass.ds(i * MT, MT)
                        dve.wait_ge(ya_hi, i + 1)
                        v.tensor_tensor(yT[:, ky, 1, :], va[:], yT[:, ky, 0, :].bitcast(F32), ALU.subtract).then_inc(ya_lo, 1)
            G0 = PAIRS * NK

            dve.wait_ge(mem_squared, PAIRS * TT)
            v.tensor_reduce(m_s1, m_ss, AX_X, ALU.add).then_inc(mem_stat, 1)
            dve.wait_ge(mem_stat, 1)
            v.tensor_scalar(m_rs, m_s1, 1.0 / D, EPS, ALU.mult, ALU.add).then_inc(mem_stat, 1)
            dve.wait_ge(mem_stat, 3)
            v.reciprocal(m_rs, m_rt).then_inc(mem_stat, 1)
            dve.wait_ge(mem_stat, 4)

            with dve.Fori(0, NG // 2) as i:
                for s in range(2):
                    cols = bass.ds(i * (2 * MW) + s * MW, MW)
                    for q in range(U_GO):
                        c = U_OUT + s * U_GO + q
                        low(i, 2 * U_GO, c + RING)
                        if q == 2:
                            dve.wait_ge(turn_done, i * 8 + KD + 4 * s)
                            for t in range(TT):
                                v.tensor_scalar(stage[:, t, :], memb[:, t, cols], m_rs[:, t:t + 1], None,
                                                ALU.mult).then_inc(mem_staged, 1)
                        if 5 <= q < 9:
                            k = q - 5
                            kc = bass.ds(i * 8 + 4 * s + k, 1)
                            turned_low(xT[:, kc, 1, :].rearrange("p a b -> p (a b)"),
                                       xT[:, kc, 0, :].rearrange("p a b -> p (a b)"),
                                       v_("mem_g", i * 8 + 4 * s + k), i * 8 + KD + 4 * s + k + 1, k)
                        if q == U_GO - 1:
                            dve.wait_ge(units_used, i * (2 * U_GO) + c + 1)
                            v.tensor_tensor(h[:, :, cols], acc[:, s], h[:, :, cols], ALU.add).then_inc(acc_freed, 1)
            G0 += NG

            def stat(total, parts, mean, count_sem, first, wait):
                v.tensor_reduce(total, parts, AX_X, ALU.add).then_inc(count_sem, 1)
                dve.wait_ge(count_sem, first + 1)
                v.tensor_scalar(mean, total, 1.0 / D, EPS, ALU.mult, ALU.add).then_inc(count_sem, 1)

            for c in range(U_KH):
                low(0, 0, U_K0 + c + RING)
                for k in h_chunks(c):
                    turned_low(hT[:, k, 1, :], hT[:, k, 0, :], v_("x_g", k), 2 * KD + k + 1, k % 4)
                if c == 6:
                    dve.wait_ge(h_squared, 2 * NG)
                    stat(h_s1, h_ss, h_rs, h_stat, 0, None)
                if c == 7:
                    dve.wait_ge(h_stat, 3)
                    v.reciprocal(h_rs, h_rt).then_inc(h_stat, 1)
                    dve.wait_ge(h_stat, 4)
                    v.tensor_scalar(h_sc, h_rs, SCORE_SCALE, None, ALU.mult).then_inc(h_stat, 1)
                    dve.wait_ge(h_stat, 5)
                if c % PU == PU - 1:
                    g = c // PU
                    add_half(kT[:, 2 * g:2 * g + 2, :], g, G0 - NG + g + 1, half_k)
            G0 += 2
            H0 = G0 - NG

            def queries_values(i, per, u, groups, halves, head):
                for c in range(U_KH + U_V):
                    low(i, per, u + c + RING)
                    if c in (PU - 1, 2 * PU - 1):
                        g = c // PU
                        add_half(qT[:, 2 * g:2 * g + 2, :], g, halves + g + 1, half_k)
                    if c == U_KH + 2:
                        dve.wait_ge(scores_done, head + 1)
                        v.tensor_reduce(s_max, aux[:, 0, :].rearrange("p (t m) -> p t m", t=TT), AX_X,
                                        ALU.max).then_inc(score_max, 1)
                        dve.wait_ge(score_max, head * 2 + 1)
                        v.scalar_tensor_tensor(out=s_nmax, in0=s_max, scalar=-1.0, in1=h_sc, op0=ALU.mult,
                                               op1=ALU.mult).then_inc(score_max, 1)
                    if c == U_KH + 3:
                        dve.wait_ge(exp_done, head * 2 + 2)
                        v.reciprocal(s_rsum, s_sum).then_inc(exp_scale, 1)
                        dve.wait_ge(exp_scale, head * 3 + 1)
                        for t in range(TT):
                            v.tensor_scalar(pp[:, t, :], pp[:, t, :], s_rsum[:, t:t + 1], None, ALU.mult).then_inc(exp_scale, 1)
                    if c == U_KH + U_V - 1:
                        dve.wait_ge(v_act, head + 1)
                        v.tensor_copy(vv[:, 1, :], acc[:, 0, 1, :]).then_inc(acc_freed, 1)

            def heads_out(head):
                for b in range(2):
                    kc = slice(head * HC + 2 * b, head * HC + 2 * b + 2) if isinstance(head, int) else bass.ds(head * HC + 2 * b, 2)
                    dve.wait_ge(o_hi, head * 2 + b + 1)
                    v.tensor_tensor(oT[:, kc, 1, :], aux[:, 2 + b, :].rearrange("p (a b) -> p a b", a=2),
                                    oT[:, kc, 0, :].bitcast(F32), ALU.subtract).then_inc(o_lo, 1)

            with dve.Fori(0, HEADS - 1) as i:
                queries_values(i, U_HEAD, U_ATT, i * 5 + G0, i * 4 + H0, i)
                for c in range(U_KH):
                    low(i, U_HEAD, U_ATT + U_KH + U_V + c + RING)
                    if c in (PU - 1, 2 * PU - 1):
                        g = c // PU
                        add_half(kT[:, 2 * g:2 * g + 2, :], 1 - g, i * 4 + H0 + 2 + g + 1, half_k)
                heads_out(i)
            G0 += 5 * (HEADS - 1)
            H0 += 4 * (HEADS - 1)
            queries_values(0, 0, U_LAST, G0, H0, HEADS - 1)
            for n in range(NG):
                for q in range(U_V):
                    u = U_WO + n * U_V + q
                    if u + RING < U_END:
                        low(0, 0, u + RING)
                    if n == 0 and q == 1:
                        heads_out(HEADS - 1)
                    if q == U_V - 1 and n < NG - 1:
                        dve.wait_ge(units_used, u + 1)
                        cols = slice(n * MW, (n + 1) * MW)
                        v.tensor_tensor(h[:, :, cols], acc[:, (n + 1) % 2], h[:, :, cols], ALU.add).then_inc(acc_freed, 1)
                        if n == 0:
                            dve.wait_ge(fg_landed, 16)
                        dve.wait_ge(acc_freed, G0 + 3 + n + 3)
                        for t in range(TT):
                            v.tensor_tensor(memb[:, t, cols], h[:, t, cols], fg[:, cols], ALU.mult).then_inc(gained, 1)
            n = NG - 1
            cols = slice(n * MW, D)
            for t in range(TT):
                if t == 0:
                    dve.wait_ge(first_tile, 1)
                else:
                    dve.wait_ge(units_used, U_END)
                v.tensor_tensor(h[:, t, cols], acc[:, (n + 1) % 2, t], h[:, t, cols], ALU.add).then_inc(h_last, 1)
                dve.wait_ge(h_last, t + 1)
                v.tensor_tensor(memb[:, t, cols], h[:, t, cols], fg[:, cols], ALU.mult).then_inc(gained, 1)
                dve.wait_ge(o_squared, n * TT + t + 1)
                v.tensor_reduce(f_s1[:, t:t + 1], f_ss[:, t], AX_X, ALU.add).then_inc(f_stat, 1)
                dve.wait_ge(f_stat, t * 4 + 1)
                v.tensor_scalar(f_ms[:, t:t + 1], f_s1[:, t:t + 1], 1.0 / D, EPS, ALU.mult, ALU.add).then_inc(f_stat, 1)
                dve.wait_ge(f_stat, t * 4 + 3)
                v.reciprocal(f_rs[:, t:t + 1], f_rt[:, t:t + 1]).then_inc(f_stat, 1)
                dve.wait_ge(f_stat, t * 4 + 4)
                dve.wait_ge(gained, n * TT + t + 1)
                for c in range(0, NG, 2):
                    oc = slice(c * MW, (c + 1) * MW)
                    v.tensor_scalar(h[:, t, oc], memb[:, t, oc], f_rs[:, t:t + 1], None, ALU.mult).then_inc(out_dve, 1)


_INS = ['x', 'mem', 'norm_mix_g', 'w_in', 'conv_a_w', 'conv_a_b', 'conv_b_w', 'conv_b_b', 'w_rgate', 'b_rgate',
        'w_igate', 'b_igate', 'lru_lambda', 'w_out', 'norm_x_g', 'norm_mem_g', 'w_q', 'w_kv', 'w_o', 'norm_f_g']


def kernel(**inputs):
    import concourse.bacc as _bacc
    from concourse.bass_utils import run_bass_kernel_spmd as _run

    nc = _bacc.Bacc("TRN2", target_bir_lowering=False, num_devices=1)
    arrays, args = {}, []
    for name in _INS:
        a = np.ascontiguousarray(inputs[name])
        arrays[f"in_{name}_dram"] = a
        args.append(nc.dram_tensor(f"in_{name}_dram", a.shape, mybir.dt.from_np(a.dtype), kind="ExternalInput").ap())
    shape = np.shape(inputs["x"])
    out = nc.dram_tensor("out_0_dram", shape, F32, kind="ExternalOutput").ap()
    hybrid_layer(nc, *args, out)
    r = _run(nc, [arrays], core_ids=[0])
    return r.results[0]["out_0_dram"]
```

```python
from contextlib import ExitStack

import numpy as np

import concourse.bass as bass
from concourse import mybir
from concourse.alu_op_type import AluOpType as ALU

F32 = mybir.dt.float32
F32R = mybir.dt.float32r
ACT = mybir.ActivationFunctionType
AX_X = mybir.AxisListType.X

P = 128
EPS = 1e-6
LRU_C = 8.0
HEADS = 4


def hybrid_layer(nc, x, mem, norm_mix_g, w_in, conv_a_w, conv_a_b, conv_b_w, conv_b_b,
                 w_rgate, b_rgate, w_igate, b_igate, lru_lambda, w_out,
                 norm_x_g, norm_mem_g, w_q, w_kv, w_o, norm_f_g, out):
    S, D = x.shape[1], x.shape[2]
    M = mem.shape[1]
    assert x.shape[0] == 1 and M == S and S == 2 * P
    TT = S // P
    KD = D // P
    KM = w_out.shape[1] // P
    UW = 1024
    PW = 256
    PK = UW // PW
    PU = KD // PK
    MW = 512
    MK = UW // MW
    MT = PW // P
    RING = 4
    HD = D // HEADS
    HC = HD // P
    SCORE_SCALE = float(HD) ** -0.5
    PAIRS = D // PW
    NG = D // MW
    KINDS = (4, 5, 0, 2, 1, 3)
    U_PAIR = len(KINDS) * PU
    U_OUT = PAIRS * U_PAIR
    U_GO = KM // MK
    U_K0 = U_OUT + NG * U_GO
    U_KH = (HD // PW) * PU
    U_V = KD // MK
    U_HEAD = U_KH + U_V + U_KH
    U_ATT = U_K0 + U_KH
    U_LAST = U_ATT + (HEADS - 1) * U_HEAD
    U_WO = U_LAST + U_KH + U_V
    U_END = U_WO + NG * U_V
    assert all(u % RING == 0 for u in (U_PAIR, U_OUT, U_GO, U_K0, U_KH, U_V, U_ATT, U_LAST, U_WO))

    TURNS_BEFORE = (range(0, 8), range(8, 12), range(12, 16), ())
    UNITS_AMID = (3, 7, 11, 15)
    SOFTPLUS_AMID = 7
    H_TURNS = (range(0, 2), range(2, 4), range(4, 6), range(6, 8), range(8, 11), range(11, 14), range(14, 16), ())
    WEIGH_LAST = 2

    xs = x[0].rearrange("(t p) d -> p t d", p=P)
    ms = mem[0].rearrange("(t p) d -> p t d", p=P)
    outs = out[0].rearrange("(t p) d -> p t d", p=P)
    rows = lambda w: w[0].rearrange("(k p) n -> p k n", p=P)
    win_r, wout_r, wq_r, wkv_r, wo_r = (rows(w) for w in (w_in, w_out, w_q, w_kv, w_o))

    with ExitStack() as ctx:
        def sb(name, shape, dt=F32, stack=ctx):
            return stack.enter_context(nc.sbuf_tensor(name, shape, dt))

        def sem(name):
            return ctx.enter_context(nc.semaphore(name))

        raw = sb("raw", [P, RING, UW])
        w_hi = sb("w_hi", [P, RING, UW], F32R)
        w_lo = sb("w_lo", [P, RING, UW], F32R)
        xT = sb("xT", [P, KD, 2, S], F32R)
        yT = sb("yT", [P, KM, 2, S], F32R)
        h = sb("h", [P, TT, D])
        ident = sb("ident", [P, P])
        vrows = sb("vrows", [P, 2, P])
        vec = sb("vec", [P, 2, P])
        small = sb("small", [P, 62 + 2 * PAIRS])
        start = sb("start", [P, 4])
        hT = yT[:, 0:KD]
        oT = yT[:, KD:2 * KD]

        vflat = vec[:, :, :].rearrange("p a b -> p (a b)")
        VN = {n: KD * k for k, n in enumerate(
            ["mix_g", "x_g", "mem_g", "aw0", "aw1", "aw2", "ab", "bw0", "bw1", "bw2", "bw3", "bb", "br", "bi", "lam"])}
        VN["decay"] = VN["lam"] + KD

        def v_(name, m):
            return vflat[:, VN[name] + m:VN[name] + m + 1] if isinstance(m, int) else vflat[:, bass.ds(m + VN[name], 1)]

        x_ss, x_ms = small[:, 72:78].rearrange("p (t n) -> p t n", t=2), small[:, 0:2]
        x_rt, x_rs = small[:, 2:4], small[:, 4:6]
        m_ss, m_s1 = small[:, 54:54 + 2 * PAIRS].rearrange("p (t n) -> p t n", t=2), small[:, 6:8]
        m_rt, m_rs = small[:, 8:10], small[:, 10:12]
        h_ss, h_s1, h_rt, h_rs, h_sc = (small[:, 12:20].rearrange("p (t n) -> p t n", t=2), small[:, 20:22],
                                        small[:, 22:24], small[:, 24:26], small[:, 26:28])
        f_ss, f_s1, f_rt, f_rs, f_ms = (small[:, 28:36].rearrange("p (t n) -> p t n", t=2), small[:, 36:38],
                                  small[:, 38:40], small[:, 40:42], small[:, 70:72])
        s_max, s_nmax, s_sum, s_rsum = small[:, 42:44], small[:, 44:46], small[:, 46:48], small[:, 48:50]

        acc = ctx.enter_context(nc.psum_tensor("acc", [P, 2, 2, 512], F32))
        aux = ctx.enter_context(nc.psum_tensor("aux", [P, 4, 512], F32))

        raw_landed = [sem(f"raw_landed{s}") for s in range(RING)]
        hi_ready = sem("hi_ready")
        raw_freed = sem("raw_freed")
        units_used = sem("units_used")
        wait_carrier = sem("wait_carrier")
        acc_freed = sem("acc_freed")
        half_ready = sem("half_ready")
        table_loaded = sem("table_loaded")
        ident_zero, ident_ready = sem("ident_zero"), sem("ident_ready")
        vrows_landed, vec_turned, vec_ready = sem("vrows_landed"), sem("vec_turned"), sem("vec_ready")
        softplus_act, softplus_pool, softplus_dve = sem("softplus_act"), sem("softplus_pool"), sem("softplus_dve")
        decay_ready = sem("decay_ready")
        x_landed = [[sem(f"x_landed{t}{c}") for c in range(2)] for t in range(TT)]
        x_stat = sem("x_stat")
        x_scaled, x_scaled_pool = [sem(f"x_scaled{t}") for t in range(TT)], sem("x_scaled_pool")
        turn_done, turn_hi, turn_lo = sem("turn_done"), sem("turn_hi"), sem("turn_lo")
        pads_zero = sem("pads_zero")
        conv_b_step = sem("conv_b_step")
        gate_w_landed, gw_hi_ready, gw_lo_ready = sem("gate_w_landed"), sem("gw_hi_ready"), sem("gw_lo_ready")
        xc_hi_ready, xc_lo_ready, gates_done = sem("xc_hi_ready"), sem("xc_lo_ready"), sem("gates_done")
        gate_sig, tanh_ready = sem("gate_sig"), sem("tanh_ready")
        one_plus_t, d_ready, s_ready = sem("one_plus_t"), sem("d_ready"), sem("s_ready")
        q_ready, a_ready = sem("q_ready"), sem("a_ready")
        mult_ready, mult_first, ixc_ready, u_ready = sem("mult_ready"), sem("mult_first"), sem("ixc_ready"), sem("u_ready")
        scanned, gb_sig, gb_silu = sem("scanned"), sem("gb_sig"), sem("gb_silu")
        yb_ready, yb_hi, yb_lo = sem("yb_ready"), sem("yb_hi"), sem("yb_lo")
        cv_ready, conv_a_step, ba_conv = sem("cv_ready"), sem("conv_a_step"), sem("ba_conv")
        ga_sig, ga_silu = sem("ga_sig"), sem("ga_silu")
        ya_ready, ya_hi, ya_lo = sem("ya_ready"), sem("ya_hi"), sem("ya_lo")
        mem_landed, mem_squared, mem_stat = sem("mem_landed"), sem("mem_squared"), sem("mem_stat")
        mem_staged = sem("mem_staged")
        h_squared, h_stat = sem("h_squared"), sem("h_stat")
        kq_hi, kq_lo = sem("kq_hi"), sem("kq_lo")
        scores_done, score_max, exp_done, exp_scale = sem("scores_done"), sem("score_max"), sem("exp_done"), sem("exp_scale")
        p_turned, pt_hi, pt_lo, v_hi_ready = sem("p_turned"), sem("pt_hi"), sem("pt_lo"), sem("v_hi_ready")
        pv_done, o_hi, o_lo = sem("pv_done"), sem("o_hi"), sem("o_lo")
        fg_landed, o_squared, f_stat = sem("fg_landed"), sem("o_squared"), sem("f_stat")
        first_tile, h_last, gained = sem("first_tile"), sem("h_last"), sem("gained")
        out_dve, out_act, stored = sem("out_dve"), sem("out_act"), sem("stored")

        with ExitStack() as with_mem:
            memb = sb("memb", [P, TT, D], stack=with_mem)
            with ExitStack() as first:
                xn = sb("xn", [P, TT, D], stack=first)
                sp = sb("sp", [P, 8, KD], stack=first)
                junk = sb("junk", [P, TT, D * 3 // 4], stack=first)
            with ExitStack() as mixer:
                def tile(name, pad=0, stack=mixer, dt=F32):
                    return sb(name, [P, MT, S + pad], dt, stack)
                half = tile("half")
                xb = tile("xb", 3)
                cv = tile("cv", 2)
                xc, g_pre = tile("xc"), tile("g_pre")
                with ExitStack() as after_gates:
                    g_sig, t2 = tile("g_sig", stack=after_gates), tile("t2", stack=after_gates)
                xc_hi, gw_hi = tile("xc_hi", dt=F32R), sb("gw_hi", [P, 2, MT, P], F32R, mixer)
                ig = tile("ig")
                with ExitStack() as after_gates:
                    dd = tile("dd", stack=after_gates)
                xc_lo = tile("xc_lo", dt=F32R)
                ss, qq, aa = (tile(n) for n in ("ss", "qq", "aa"))
                with ExitStack() as after_gates:
                    va = tile("va", stack=after_gates)
                gw_lo = sb("gw_lo", [P, 2, MT, P], F32R, mixer)
                gw = sb("gw", [P, 2, MT, P], stack=mixer)
                ba, ca, conv_a = t2, dd, ss
            with ExitStack() as later:
                stage = sb("stage", [P, TT, MW], stack=later)
                junk_a = sb("junk_a", [P, MW], stack=later)
        k_lo = sb("k_lo", [P, HC, M], F32R)
        q_lo = sb("q_lo", [P, HC, S], F32R)
        v_lo = sb("v_lo", [P, TT, HD], F32R)
        pT_lo = sb("pT_lo", [P, TT, S], F32R)
        half_k = sb("half_k", [P, MT, S])
        assert HC * (M + S) + TT * (HD + S) + MT * S == TT * D
        k_hi = sb("k_hi", [P, HC, M], F32R)
        q_hi = sb("q_hi", [P, HC, S], F32R)
        v_hi = sb("v_hi", [P, TT, HD], F32R)
        pT_hi = sb("pT_hi", [P, TT, S], F32R)
        pp = sb("pp", [P, TT, M])
        fg = sb("fg", [P, D])
        junk_o = pp[:, :, :].rearrange("p a b -> p (a b)")

        block = ctx.enter_context(nc.Block())

        @block.sync
        def _(sp_):
            for c in range(2):
                for t in range(TT):
                    sp_.dma_start(h[:, t, c * (D // 2):(c + 1) * (D // 2)],
                                  xs[:, t, c * (D // 2):(c + 1) * (D // 2)]).then_inc(x_landed[t][c], 16)

            at = 0
            for src in (norm_mix_g, norm_x_g, norm_mem_g, conv_a_w[0], conv_a_b, conv_b_w[0], conv_b_b,
                        b_rgate, b_igate, lru_lambda):
                r = src.rearrange("k (m c) -> (k m) c", c=P)
                done = 0
                while done < r.shape[0]:
                    k = min(r.shape[0] - done, P - at % P)
                    sp_.dma_start(vrows[at % P:at % P + k, at // P, :], r[done:done + k, :]).then_inc(vrows_landed, 16)
                    at, done = at + k, done + k

            def unit(i, per, c, w, k0, nk, base, col, width):
                first_column = base + col
                if not isinstance(base, int):
                    first_column = sp_.snap(first_column)
                sp_.wait_ge(raw_freed, i * per + c + 1)
                if not isinstance(base, int) and k0 == col == 0:
                    sp_.sem_inc(wait_carrier, 1)
                dst = raw[:, c % RING, :].rearrange("p (k n) -> p k n", k=nk)
                src = w[:, k0:k0 + nk, bass.ds(first_column, width)]
                sp_.dma_start(dst, src).then_inc(raw_landed[c % RING], 16)

            with sp_.Fori(0, PAIRS) as i:
                for g, kind in enumerate(KINDS):
                    for q in range(PU):
                        unit(i, U_PAIR, g * PU + q, win_r, q * PK, PK, i * PW, kind * D, PW)
            with sp_.Fori(0, NG // 2) as i:
                for s in range(2):
                    for q in range(U_GO):
                        unit(i, 2 * U_GO, U_OUT + s * U_GO + q, wout_r, q * MK, MK, i * (2 * MW), s * MW, MW)

            def keys(i, per, u, base, col, w):
                for g in range(HD // PW):
                    for q in range(PU):
                        unit(i, per, u + g * PU + q, w, q * PK, PK, base, col + g * PW, PW)

            def values(i, per, u, base, col, w):
                for q in range(U_V):
                    unit(i, per, u + q, w, q * MK, MK, base, col, MW)

            keys(0, 0, U_K0, 0, 0, wkv_r)
            with sp_.Fori(0, HEADS - 1) as i:
                keys(i, U_HEAD, U_ATT, i * HD, 0, wq_r)
                values(i, U_HEAD, U_ATT + U_KH, i * HD, D, wkv_r)
                keys(i, U_HEAD, U_ATT + U_KH + U_V, i * HD, HD, wkv_r)
            keys(0, 0, U_LAST, 0, (HEADS - 1) * HD, wq_r)
            values(0, 0, U_LAST + U_KH, 0, D + (HEADS - 1) * HD, wkv_r)
            for n in range(NG):
                values(0, 0, U_WO + n * U_V, 0, n * MW, wo_r)

            for t in range(TT):
                for c in range(NG):
                    sp_.wait_ge((out_dve, out_act)[c % 2], t * (NG // 2) + c // 2 + 1)
                    cols = slice(c * MW, (c + 1) * MW)
                    sp_.dma_start(outs[:, t, cols], h[:, t, cols]).then_inc(stored, 16)
            sp_.wait_ge(stored, 16 * TT * NG)

        @block.gpsimd
        def _(pool):
            pool.memset(ident[:], 0.0).then_inc(ident_zero, 1)
            pool.wait_ge(ident_zero, 1)
            pool.affine_select(out=ident[:], in_=ident[:], compare_op=ALU.not_equal, fill=1.0, base=0,
                               pattern=[[-1, P]], channel_multiplier=1).then_inc(ident_ready, 1)

            def chain(ins):
                steps[0] += 1
                ins.then_inc(softplus_pool, 1)
                pool.wait_ge(softplus_pool, steps[0])

            def gate_weights(head):
                heads = slice(head, head + MT) if isinstance(head, int) else bass.ds(head, MT)
                for k, w in enumerate((w_rgate, w_igate)):
                    pool.dma_start(gw[:, k], w[0, heads].rearrange("m i j -> i m j")).then_inc(gate_w_landed, 16)

            pool.wait_ge(x_stat, 10)
            for c in range(D // 2, D, MW):
                nc.gpsimd.tensor_scalar(xn[:, 1, c:c + MW], h[:, 1, c:c + MW], x_rs[:, 1:2], None,
                                        ALU.mult).then_inc(x_scaled_pool, 1)
            gate_weights(0)

            z, den, inv, r, r2, poly, neg = (sp[:, k, :] for k in range(1, 8))
            lam = vflat[:, VN["lam"]:VN["lam"] + KD]
            steps = [0]
            pool.wait_ge(softplus_act, 2)
            chain(nc.gpsimd.tensor_scalar(den, z, 1.0, 2.0, ALU.mult, ALU.add))
            pool.wait_ge(softplus_dve, 1)
            chain(nc.gpsimd.tensor_tensor(r, z, inv, ALU.mult))
            chain(nc.gpsimd.tensor_tensor(r2, r, r, ALU.mult))
            chain(nc.gpsimd.tensor_scalar(poly, r2, 1.0 / 19, 1.0 / 17, ALU.mult, ALU.add))
            for k in range(15, 0, -2):
                chain(nc.gpsimd.tensor_tensor(poly, poly, r2, ALU.mult))
                chain(nc.gpsimd.tensor_scalar(poly, poly, 1.0, 1.0 / k, ALU.mult, ALU.add))
            chain(nc.gpsimd.tensor_tensor(poly, poly, r, ALU.mult))
            chain(nc.gpsimd.tensor_scalar(neg, lam, -1.0, 0.0, ALU.mult, ALU.max))
            chain(nc.gpsimd.tensor_scalar(neg, neg, LRU_C / 2, 0.0, ALU.mult, ALU.add))
            chain(nc.gpsimd.tensor_scalar(poly, poly, LRU_C, 0.0, ALU.mult, ALU.add))
            nc.gpsimd.tensor_tensor(vflat[:, VN["decay"]:VN["decay"] + KD], poly, neg, ALU.add).then_inc(decay_ready, 1)

            def mem_columns(i):
                cols = bass.ds(i * PW, PW)
                pool.dma_start(memb[:, :, cols], ms[:, :, cols]).then_inc(mem_landed, 16)

            pool.wait_ge(units_used, 2 * PU)
            mem_columns(0)
            with pool.Fori(1, PAIRS) as i:
                pool.wait_ge(gates_done, i)
                gate_weights(i * MT)
                pool.wait_ge(mem_squared, i * TT)
                mem_columns(i)
            pool.wait_ge(turn_lo, 3 * KD)
            pool.dma_start(fg[:], norm_f_g.rearrange("(o d) -> o d", o=1).to_broadcast([P, D])).then_inc(fg_landed, 16)

        @block.tensor
        def _(pe):
            def project_unit(i, per, c, src, a, q):
                s = c % RING
                pe.wait_ge(raw_freed, i * per + c + 1 + RING)
                for kk in range(PK):
                    kc = q * PK + kk
                    for m in range(MT):
                        wh = w_hi[:, s, kk * PW + m * P:kk * PW + (m + 1) * P]
                        wl = w_lo[:, s, kk * PW + m * P:kk * PW + (m + 1) * P]
                        both = (acc[:, a, m, :], wh, src[:, kc].rearrange("p a b -> p (a b)"))
                        high = (acc[:, a, m, 0:S], wl, src[:, kc, 0, :])
                        last = kc == KD - 1
                        for o, l, r in ((high, both) if last else (both, high)):
                            mm = nc.tensor.matmul(o, l, r, start=kc == 0 and l is wh, stop=last and l is wh)
                mm.then_inc(units_used, 1)

            def mix_unit(i, per, c, src, a, q, nk, tiles=range(TT)):
                s = c % RING
                pe.wait_ge(raw_freed, i * per + c + 1 + RING)
                for kk in range(MK):
                    kc = q * MK + kk
                    wh, wl = (w[:, s, kk * MW:(kk + 1) * MW] for w in (w_hi, w_lo))
                    for t in tiles:
                        o = acc[:, a, t, :]
                        hi, lo = (src[:, kc, k, t * P:(t + 1) * P] for k in range(2))
                        nc.tensor.matmul(o, hi, wh, start=kc == 0, stop=False)
                        nc.tensor.matmul(o, hi, wl, start=False, stop=False)
                        mm = nc.tensor.matmul(o, lo, wh, start=False, stop=kc == nk - 1)
                if TT - 1 in tiles:
                    mm.then_inc(units_used, 1)
                return mm

            def turn(src, c):
                for t in range(TT):
                    mm = nc.tensor.transpose(aux[:, c % 4, t * P:(t + 1) * P], src[:, t, c * P:(c + 1) * P], ident[:])
                mm.then_inc(turn_done, 1)

            pe.wait_ge(ident_ready, 1)
            pe.wait_ge(vrows_landed, 16 * 11)
            for k in range(2):
                rows_k = P if k == 0 else (15 * KD - P)
                mm = nc.tensor.transpose(aux[:, 0, k * P:k * P + rows_k], vrows[0:rows_k, k, :], ident[0:rows_k, 0:rows_k])
            mm.then_inc(vec_turned, 1)

            def pair(i, first):
                for g in range(len(KINDS)):
                    pe.wait_ge(acc_freed, i * len(KINDS) + g + 1)
                    for q in range(PU):
                        c = g * PU + q
                        if first and c == 0:
                            pe.wait_ge(vec_ready, 1)
                        for k in (TURNS_BEFORE[c] if first and c < PU else ()):
                            if k % 4 == 0:
                                pe.wait_ge(x_scaled[0], k // 4 + 1)
                                if k < KD // 2:
                                    pe.wait_ge(x_scaled[1], k // 4 + 1)
                                else:
                                    pe.wait_ge(x_scaled_pool, (k - KD // 2) // 4 + 1)
                            if k >= 4:
                                pe.wait_ge(turn_lo, k - 3)
                            turn(xn, k)
                        if first and c < PU:
                            pe.wait_ge(turn_lo, (c + 1) * PK)
                        project_unit(i, U_PAIR, c, xT, g % 2, q)
                        if c == 8:
                            pe.wait_ge(gw_lo_ready, i + 1)
                            pe.wait_ge(xc_lo_ready, i + 1)
                            for k in range(2):
                                for m in range(MT):
                                    o = aux[:, k, m * S:(m + 1) * S]
                                    nc.tensor.matmul(o, gw_hi[:, k, m, :], xc_hi[:, m, :], start=True, stop=False)
                                    nc.tensor.matmul(o, gw_hi[:, k, m, :], xc_lo[:, m, :], start=False, stop=False)
                                    mm = nc.tensor.matmul(o, gw_lo[:, k, m, :], xc_hi[:, m, :], start=False, stop=True)
                            mm.then_inc(gates_done, 1)

            pair(0, True)
            with pe.Fori(1, PAIRS) as i:
                pair(i, False)
            G0 = PAIRS * len(KINDS)

            with pe.Fori(0, NG // 2) as i:
                for s in range(2):
                    pe.wait_ge(acc_freed, i * 2 + G0 + s + 1)
                    for q in range(U_GO):
                        if s == 0 and q == KD // MK - 1:
                            pe.wait_ge(ya_lo, PAIRS)
                        if s == 0 and q == U_GO - 1:
                            pe.wait_ge(yb_lo, PAIRS)
                        mix_unit(i, 2 * U_GO, U_OUT + s * U_GO + q, yT, s, q, KM)
                        if 4 <= q < 8:
                            if q == 4:
                                pe.wait_ge(mem_staged, i * 4 + 2 * s + 2)
                            pe.wait_ge(turn_lo, i * 8 + KD + 4 * s + (q - 4) - 3)
                            for t in range(TT):
                                mm = nc.tensor.transpose(aux[:, q - 4, t * P:(t + 1) * P],
                                                         stage[:, t, (q - 4) * P:(q - 3) * P], ident[:])
                            mm.then_inc(turn_done, 1)
            G0 += NG

            pe.wait_ge(turn_lo, 2 * KD)
            for g in range(2):
                pe.wait_ge(acc_freed, G0 + g + 1)
                for q in range(PU):
                    project_unit(0, 0, U_K0 + g * PU + q, xT, g, q)
                    for c in H_TURNS[g * PU + q]:
                        if c % 4 == 0:
                            pe.wait_ge(acc_freed, G0 - NG + c // 4 + 3)
                        pe.wait_ge(turn_lo, 2 * KD + c - 3)
                        turn(h, c)
            G0 += 2

            def scores(halves):
                pe.wait_ge(kq_lo, halves + 4)
                for t in range(TT):
                    tile_ = slice(t * P, (t + 1) * P)
                    for d in range(HC):
                        o = aux[:, 0, t * M:(t + 1) * M]
                        nc.tensor.matmul(o, q_hi[:, d, tile_], k_hi[:, d, :], start=d == 0, stop=False)
                        nc.tensor.matmul(o, q_hi[:, d, tile_], k_lo[:, d, :], start=False, stop=False)
                        mm = nc.tensor.matmul(o, q_lo[:, d, tile_], k_hi[:, d, :], start=False, stop=d == HC - 1)
                mm.then_inc(scores_done, 1)

            def turn_p(i):
                pe.wait_ge(exp_scale, i * 3 + 3)
                for mk in range(TT):
                    for t in range(TT):
                        mm = nc.tensor.transpose(aux[:, 1, mk * S + t * P:mk * S + (t + 1) * P],
                                                 pp[:, t, mk * P:(mk + 1) * P], ident[:])
                mm.then_inc(p_turned, 1)

            def weigh_values(i, groups):
                pe.wait_ge(pt_lo, i + 1)
                pe.wait_ge(acc_freed, groups + 5)
                for d in range(HC):
                    o = aux[:, 2 + d // 2, (d % 2) * S:(d % 2 + 1) * S]
                    for mk in range(TT):
                        vh, vl = (w[:, mk, d * P:(d + 1) * P] for w in (v_hi, v_lo))
                        nc.tensor.matmul(o, vh, pT_hi[:, mk, :], start=mk == 0, stop=False)
                        nc.tensor.matmul(o, vh, pT_lo[:, mk, :], start=False, stop=False)
                        mm = nc.tensor.matmul(o, vl, pT_hi[:, mk, :], start=False, stop=mk == TT - 1)
                mm.then_inc(pv_done, 1)

            def queries_values(i, per, u, groups, head):
                for g in range(2):
                    pe.wait_ge(acc_freed, groups + g + 1)
                    for q in range(PU):
                        project_unit(i, per, u + g * PU + q, hT, g, q)
                pe.wait_ge(acc_freed, groups + 3)
                for q in range(U_V):
                    mix_unit(i, per, u + U_KH + q, xT, 0, q, KD)
                    if q == 1:
                        scores(head * 4)
                    if q == 5:
                        turn_p(head)

            pe.wait_ge(turn_lo, 3 * KD)
            with pe.Fori(0, HEADS - 1) as i:
                queries_values(i, U_HEAD, U_ATT, i * 5 + G0, i)
                for g in range(2):
                    a = 1 - g
                    pe.wait_ge(acc_freed, i * 5 + G0 + 3 + g + 1)
                    for q in range(PU):
                        project_unit(i, U_HEAD, U_ATT + U_KH + U_V + g * PU + q, xT, a, q)
                weigh_values(i, i * 5 + G0)
                pe.wait_ge(acc_freed, i * 5 + G0 + 7)
            G0 += 5 * (HEADS - 1)
            queries_values(0, 0, U_LAST, G0, HEADS - 1)
            G0 += 3
            for n in range(NG):
                pe.wait_ge(acc_freed, G0 + n + 1)
                for q in range(U_V):
                    if n == NG - 1 and q == U_V - RING:
                        for t in range(TT):
                            for k in range(q, U_V):
                                mm = mix_unit(0, 0, U_WO + n * U_V + k, oT, (n + 1) % 2, k, KD, [t])
                            if t == 0:
                                mm.then_inc(first_tile, 1)
                        break
                    if n == 0:
                        pe.wait_ge(o_lo, 2 * ((q * MK) // HC + 1))
                    mix_unit(0, 0, U_WO + n * U_V + q, oT, (n + 1) % 2, q, KD)
                    if n == 0 and q == WEIGH_LAST:
                        weigh_values(HEADS - 1, G0 - 3)

        @block.scalar
        def _(act):
            def high(i, per, c):
                s = c % RING
                act.wait_ge(raw_landed[s], i * (per // RING * 16) + (c // RING + 1) * 16)
                if c >= RING:
                    act.wait_ge(units_used, i * per + c + 1 - RING)
                nc.scalar.activation(w_hi[:, s, :], raw[:, s, :], ACT.Copy).then_inc(hi_ready, 1)

            act.wait_ge(raw_freed, RING)
            nc.scalar.activation(start[:, 2:3], start[:, 0:1], ACT.Sqrt).then_inc(table_loaded, 1)
            for part, cols in enumerate((slice(0, D // 2), slice(D * 3 // 4, D))):
                for t in range(TT):
                    act.wait_ge(x_landed[t][part], 16)
                    into = junk[:, t, 0:D // 2] if part == 0 else junk[:, t, D // 2:]
                    nc.scalar.activation(into, h[:, t, cols], ACT.Square,
                                         accum_out=x_ss[:, t, 2 * part:2 * part + 1]).then_inc(x_stat, 1)
            act.wait_ge(x_stat, 8)
            nc.scalar.activation(x_rt, x_ms, ACT.Sqrt).then_inc(x_stat, 1)
            act.wait_ge(x_stat, 10)
            for c in range(0, D // 2, MW):
                nc.scalar.activation(xn[:, 1, c:c + MW], h[:, 1, c:c + MW], ACT.Copy,
                                     scale=x_rs[:, 1:2]).then_inc(x_scaled[1], 1)
            act.wait_ge(vec_ready, 1)

            def turned_high(dst, gain, count, bank):
                act.wait_ge(turn_done, count)
                nc.scalar.activation(dst, aux[:, bank, 0:S], ACT.Copy, scale=gain).then_inc(turn_hi, 1)

            def softplus_exp():
                lam = vflat[:, VN["lam"]:VN["lam"] + KD]
                nc.scalar.activation(sp[:, 0, :], lam, ACT.Abs).then_inc(softplus_act, 1)
                act.wait_ge(softplus_act, 1)
                nc.scalar.activation(sp[:, 1, :], sp[:, 0, :], ACT.Exp, scale=-1.0).then_inc(softplus_act, 1)

            for c in range(KD):
                turned_high(xT[:, c, 0, :], v_("mix_g", c), c + 1, c % 4)
                if c in UNITS_AMID:
                    high(0, 0, UNITS_AMID.index(c))
                if c == SOFTPLUS_AMID:
                    softplus_exp()

            def copy_half(dst, a, freed):
                act.wait_ge(acc_freed, freed)
                nc.scalar.activation(dst[:], acc[:, a, :, S:2 * S], ACT.Copy).then_inc(half_ready, 1)

            with act.Fori(0, PAIRS) as i:
                for c in range(U_PAIR):
                    high(i, U_PAIR, c + RING)
                    g = c // PU
                    if c % PU == PU - 1:
                        copy_half(half, g % 2, i * len(KINDS) + 2 + g)
                    if c == 4:
                        act.wait_ge(gate_w_landed, i * 32 + 32)
                        nc.scalar.activation(gw_hi[:], gw[:], ACT.Copy).then_inc(gw_hi_ready, 1)
                    if c == 5:
                        act.wait_ge(conv_b_step, i * 8 + 8)
                        nc.scalar.activation(xc_hi[:], xc[:], ACT.Copy).then_inc(xc_hi_ready, 1)
                    if c == 9:
                        act.wait_ge(gates_done, i + 1)
                        for m in range(MT):
                            nc.scalar.activation(t2[:, m, :], aux[:, 0, m * S:(m + 1) * S], ACT.Sigmoid,
                                                 bias=v_("br", i * MT + m)).then_inc(gate_sig, 1)
                            nc.scalar.activation(ig[:, m, :], aux[:, 1, m * S:(m + 1) * S], ACT.Sigmoid,
                                                 bias=v_("bi", i * MT + m)).then_inc(gate_sig, 1)
                        act.wait_ge(gate_sig, i * 4 + 4)
                        act.wait_ge(decay_ready, 1)
                        for m in range(MT):
                            nc.scalar.activation(t2[:, m, :], t2[:, m, :], ACT.Tanh,
                                                 scale=v_("decay", i * MT + m)).then_inc(tanh_ready, 1)
                    if c == 10:
                        act.wait_ge(acc_freed, i * len(KINDS) + 4)
                        nc.scalar.activation(g_sig[:], g_pre[:], ACT.Sigmoid).then_inc(gb_sig, 1)
                    if c == 13:
                        act.wait_ge(q_ready, i + 1)
                        nc.scalar.activation(qq[:], qq[:], ACT.Sqrt, scale=-4.0).then_inc(mult_ready, 1)
                    if c in (16, 20):
                        t = (c - 16) // 4
                        if c == 16:
                            act.wait_ge(mem_landed, i * 16 + 16)
                        nc.scalar.activation(aux[:, 2 + t, 0:PW], memb[:, t, bass.ds(i * PW, PW)], ACT.Square,
                                             accum_out=m_ss[:, t, bass.ds(i, 1)]).then_inc(mem_squared, 1)
                        act.wait_ge(mem_squared, i * TT + t + 1)
                    if c == 15:
                        act.wait_ge(yb_ready, i + 1)
                        nc.scalar.activation(yT[:, bass.ds(i * MT + KD, MT), 0, :], qq[:], ACT.Copy).then_inc(yb_hi, 1)
                    if c == 23:
                        act.wait_ge(acc_freed, i * len(KINDS) + 8)
                        nc.scalar.activation(g_sig[:], g_pre[:], ACT.Sigmoid).then_inc(ga_sig, 1)
                        act.wait_ge(ya_ready, i + 1)
                        nc.scalar.activation(yT[:, bass.ds(i * MT, MT), 0, :], va[:], ACT.Copy).then_inc(ya_hi, 1)
            HALVES = PAIRS * len(KINDS)

            act.wait_ge(mem_stat, 2)
            nc.scalar.activation(m_rt, m_rs, ACT.Sqrt).then_inc(mem_stat, 1)

            with act.Fori(0, NG // 2) as i:
                for s in range(2):
                    for q in range(U_GO):
                        c = U_OUT + s * U_GO + q
                        high(i, 2 * U_GO, c + RING)
                        if 5 <= q < 9:
                            k = q - 5
                            turned_high(xT[:, bass.ds(i * 8 + 4 * s + k, 1), 0, :].rearrange("p a b -> p (a b)"),
                                        v_("mem_g", i * 8 + 4 * s + k), i * 8 + KD + 4 * s + k + 1, k)
                        if q == U_GO - 1:
                            act.wait_ge(acc_freed, i * 2 + HALVES + s + 3)
                            for t in range(TT):
                                nc.scalar.activation(junk_a[:], h[:, t, bass.ds(i * (2 * MW) + s * MW, MW)], ACT.Square,
                                                     accum_out=h_ss[:, t, bass.ds(i * 2 + s, 1)]).then_inc(h_squared, 1)
                                act.wait_ge(h_squared, i * 4 + 2 * s + t + 1)

            def split_half(a, freed, dst, halves, unit=None):
                if not isinstance(halves, int) or halves > 0:
                    act.wait_ge(kq_lo, halves)
                copy_half(half_k, a, freed)
                if unit is not None:
                    high(*unit)
                act.wait_ge(acc_freed, freed + 1)
                nc.scalar.activation(dst, half_k[:], ACT.Copy).then_inc(kq_hi, 1)

            for c in range(U_KH):
                for k in H_TURNS[c]:
                    turned_high(hT[:, k, 0, :], v_("x_g", k), 2 * KD + k + 1, k % 4)
                high(0, 0, U_K0 + c + RING)
                if c == 6:
                    act.wait_ge(h_stat, 2)
                    nc.scalar.activation(h_rt, h_rs, ACT.Sqrt).then_inc(h_stat, 1)
                if c % PU == PU - 1:
                    split_half(c // PU, HALVES + NG + 2 + c // PU, k_hi[:, 2 * (c // PU):2 * (c // PU) + 2, :], c // PU)

            def softmax(i):
                act.wait_ge(score_max, i * 2 + 2)
                for t in range(TT):
                    nc.scalar.activation(pp[:, t, :], aux[:, 0, t * M:(t + 1) * M], ACT.Exp, bias=s_nmax[:, t:t + 1],
                                         scale=h_sc[:, t:t + 1], accum_out=s_sum[:, t:t + 1]).then_inc(exp_done, 1)

            def queries_values(i, per, u, groups, head):
                for c in range(U_KH + U_V):
                    high(i, per, u + c + RING)
                    if c in (PU - 1, 2 * PU - 1):
                        g = c // PU
                        split_half(g, groups + 2 + g, q_hi[:, 2 * g:2 * g + 2, :], head * 4 + 2 + g)
                    if c == U_KH + 2:
                        softmax(head)
                    if c == U_KH + 6:
                        act.wait_ge(p_turned, head + 1)
                        nc.scalar.activation(pT_hi[:].rearrange("p a b -> p (a b)"), aux[:, 1, :], ACT.Copy).then_inc(pt_hi, 1)
                    if c == U_KH + U_V - 1:
                        for t in range(TT):
                            nc.scalar.activation(v_hi[:, t, :], acc[:, 0, t, :], ACT.Copy).then_inc(v_hi_ready, 1)

            def heads_out(head):
                act.wait_ge(pv_done, head + 1)
                for b in range(2):
                    o = oT[:, bass.ds(head * HC + 2 * b, 2), 0, :] if not isinstance(head, int) else \
                        oT[:, head * HC + 2 * b:head * HC + 2 * b + 2, 0, :]
                    nc.scalar.activation(o, aux[:, 2 + b, :].rearrange("p (a b) -> p a b", a=2), ACT.Copy).then_inc(o_hi, 1)

            G0 = HALVES + NG + 2
            with act.Fori(0, HEADS - 1) as i:
                queries_values(i, U_HEAD, U_ATT, i * 5 + G0, i)
                for c in range(U_KH):
                    unit = (i, U_HEAD, U_ATT + U_KH + U_V + c + RING)
                    if c in (PU - 1, 2 * PU - 1):
                        g = c // PU
                        act.wait_ge(units_used, i * U_HEAD + U_ATT + U_KH + U_V + c + 1)
                        split_half(1 - g, i * 5 + G0 + 3 + 2 + g, k_hi[:, 2 * g:2 * g + 2, :], i * 4 + 4 + g, unit)
                    else:
                        high(*unit)
                heads_out(i)
            G0 += 5 * (HEADS - 1)
            queries_values(0, 0, U_LAST, G0, HEADS - 1)
            for n in range(NG):
                for q in range(U_V):
                    u = U_WO + n * U_V + q
                    if u + RING < U_END:
                        high(0, 0, u + RING)
                    if n == 0 and q == WEIGH_LAST:
                        heads_out(HEADS - 1)
                    if q == U_V - 1 and n < NG - 1:
                        act.wait_ge(acc_freed, G0 + 3 + n + 3)
                        for t in range(TT):
                            if n + t:
                                act.wait_ge(o_squared, n * TT + t)
                            nc.scalar.activation(junk_o[:], h[:, t, n * MW:(n + 1) * MW], ACT.Square,
                                                 accum_out=f_ss[:, t, n:n + 1]).then_inc(o_squared, 1)
                        if n == 0:
                            nc.scalar.activation(start[:, 3:4], start[:, 0:1], ACT.Sqrt).then_inc(table_loaded, 1)
            n = NG - 1
            for t in range(TT):
                act.wait_ge(h_last, t + 1)
                act.wait_ge(o_squared, n * TT + t)
                nc.scalar.activation(junk_o[:], h[:, t, n * MW:(n + 1) * MW], ACT.Square,
                                     accum_out=f_ss[:, t, n:n + 1]).then_inc(o_squared, 1)
                act.wait_ge(f_stat, t * 4 + 2)
                nc.scalar.activation(f_rt[:, t:t + 1], f_ms[:, t:t + 1], ACT.Sqrt).then_inc(f_stat, 1)
                act.wait_ge(f_stat, t * 4 + 4)
                for c in range(1, NG, 2):
                    cols = slice(c * MW, (c + 1) * MW)
                    nc.scalar.activation(h[:, t, cols], memb[:, t, cols], ACT.Copy, scale=f_rs[:, t:t + 1]).then_inc(out_act, 1)

        @block.vector
        def _(dve):
            v = nc.vector

            def low(i, per, c):
                s = c % RING
                dve.wait_ge(hi_ready, i * per + c + 1)
                v.tensor_tensor(w_lo[:, s, :], raw[:, s, :], w_hi[:, s, :].bitcast(F32), ALU.subtract).then_inc(raw_freed, 1)

            v.memset(start[:, 0:1], 0.0).then_inc(raw_freed, RING)
            v.memset(start[:, 1:2], 0.0).then_inc(acc_freed, 2)
            third = slice(D // 2, D * 3 // 4)
            for t in range(TT):
                dve.wait_ge(x_landed[t][1], 16)
                v.tensor_tensor_reduce(xn[:, t, 0:D // 4], h[:, t, third], h[:, t, third], 1.0, 0.0, ALU.mult,
                                       ALU.add, x_ss[:, t, 1:2]).then_inc(x_stat, 1)
            dve.wait_ge(x_stat, 6)
            v.tensor_reduce(x_ms, x_ss, AX_X, ALU.add).then_inc(x_stat, 1)
            dve.wait_ge(x_stat, 7)
            v.tensor_scalar(x_ms, x_ms, 1.0 / D, EPS, ALU.mult, ALU.add).then_inc(x_stat, 1)
            dve.wait_ge(x_stat, 9)
            v.reciprocal(x_rs, x_rt).then_inc(x_stat, 1)
            dve.wait_ge(vec_turned, 1)
            v.tensor_copy(vflat[:, 0:15 * KD], aux[:, 0, 0:15 * KD]).then_inc(vec_ready, 1)
            dve.wait_ge(x_stat, 10)
            for c in range(0, D, MW):
                v.tensor_scalar(xn[:, 0, c:c + MW], h[:, 0, c:c + MW], x_rs[:, 0:1], None, ALU.mult).then_inc(x_scaled[0], 1)

            def turned_low(dst, hi, gain, count, bank):
                dve.wait_ge(turn_hi, count)
                v.scalar_tensor_tensor(out=dst, in0=aux[:, bank, 0:S], scalar=gain, in1=hi.bitcast(F32),
                                       op0=ALU.mult, op1=ALU.subtract).then_inc(turn_lo, 1)

            for c in range(KD):
                turned_low(xT[:, c, 1, :], xT[:, c, 0, :], v_("mix_g", c), c + 1, c % 4)
                if c in UNITS_AMID:
                    low(0, 0, UNITS_AMID.index(c))
                if c == SOFTPLUS_AMID + 4:
                    dve.wait_ge(softplus_pool, 1)
                    v.reciprocal(sp[:, 3, :], sp[:, 2, :]).then_inc(softplus_dve, 1)
            v.memset(xb[:, :, 0:3], 0.0).then_inc(pads_zero, 1)
            v.memset(cv[:, :, 0:2], 0.0).then_inc(pads_zero, 1)
            dve.wait_ge(pads_zero, 2)

            def add_half(dst, a, halves, half_tile):
                dve.wait_ge(half_ready, halves)
                v.tensor_tensor(dst, acc[:, a, :, 0:S], half_tile[:], ALU.add).then_inc(acc_freed, 1)

            NK = len(KINDS)
            with dve.Fori(0, PAIRS) as i:
                def freed(g):
                    dve.wait_ge(acc_freed, i * NK + g + 3)

                for c in range(U_PAIR):
                    low(i, U_PAIR, c + RING)
                    if c == 3:
                        add_half(xb[:, :, 3:S + 3], 0, i * NK + 1, half)
                        freed(0)
                    if c in (3, 4):
                        for k in range(2 * (c - 3), 2 * (c - 3) + 2):
                            for m in range(MT):
                                if k == 0:
                                    v.tensor_scalar(xc[:, m, :], xb[:, m, 0:S], v_("bw0", i * MT + m),
                                                    v_("bb", i * MT + m), ALU.mult, ALU.add).then_inc(conv_b_step, 1)
                                else:
                                    dve.wait_ge(conv_b_step, i * 8 + MT * (k - 1) + m + 1)
                                    v.scalar_tensor_tensor(out=xc[:, m, :], in0=xb[:, m, k:k + S],
                                                           scalar=v_(f"bw{k}", i * MT + m), in1=xc[:, m, :],
                                                           op0=ALU.mult, op1=ALU.add).then_inc(conv_b_step, 1)
                    if c == 5:
                        dve.wait_ge(gw_hi_ready, i + 1)
                        v.tensor_tensor(gw_lo[:], gw[:], gw_hi[:].bitcast(F32), ALU.subtract).then_inc(gw_lo_ready, 1)
                    if c == 6:
                        dve.wait_ge(decay_ready, 1)
                        dve.wait_ge(xc_hi_ready, i + 1)
                        v.tensor_tensor(xc_lo[:], xc[:], xc_hi[:].bitcast(F32), ALU.subtract).then_inc(xc_lo_ready, 1)
                    if c == 7:
                        dve.wait_ge(half_ready, i * NK + 2)
                        v.tensor_tensor(g_pre[:], acc[:, 1, :, 0:S], half[:], ALU.add).then_inc(acc_freed, 1)
                    if c == 10:
                        dve.wait_ge(tanh_ready, i * 2 + 2)
                        v.tensor_scalar(dd[:], t2[:], 1.0, None, ALU.add).then_inc(one_plus_t, 1)
                        dve.wait_ge(one_plus_t, i + 1)
                    if c in range(10, 10 + MT):
                        v.reciprocal(dd[:, c - 10, :], dd[:, c - 10, :]).then_inc(d_ready, 1)
                    if c == 12:
                        dve.wait_ge(d_ready, i * MT + MT)
                        v.tensor_tensor(ss[:], t2[:], dd[:], ALU.mult).then_inc(s_ready, 1)
                        dve.wait_ge(s_ready, i + 1)
                        v.scalar_tensor_tensor(out=qq[:], in0=ss[:], scalar=1.0, in1=ss[:], op0=ALU.subtract,
                                               op1=ALU.mult).then_inc(q_ready, 1)
                        v.tensor_scalar(aa[:], ss[:], -2.0, 1.0, ALU.mult, ALU.add).then_inc(a_ready, 1)
                        v.tensor_tensor(ig[:], ig[:], xc[:], ALU.mult).then_inc(ixc_ready, 1)
                    if c == 11:
                        add_half(va[:], 0, i * NK + 3, half)
                    if c == 14:
                        dve.wait_ge(mult_ready, i + 1)
                        v.memset(qq[:, :, 0:1], 1.0).then_inc(mult_first, 1)
                        dve.wait_ge(mult_first, i + 1)
                        dve.wait_ge(ixc_ready, i + 1)
                        v.tensor_tensor(ig[:], ig[:], qq[:], ALU.mult).then_inc(u_ready, 1)
                        dve.wait_ge(u_ready, i + 1)
                        dve.wait_ge(a_ready, i + 1)
                        for m in range(MT):
                            v.tensor_tensor_scan(dd[:, m, :], aa[:, m, :], ig[:, m, :], 0.0, ALU.mult,
                                                 ALU.add).then_inc(scanned, 1)
                    if c == 14:
                        dve.wait_ge(gb_sig, i + 1)
                        v.tensor_tensor(g_pre[:], g_pre[:], g_sig[:], ALU.mult).then_inc(gb_silu, 1)
                        dve.wait_ge(gb_silu, i + 1)
                        dve.wait_ge(scanned, i * 2 + 2)
                        v.tensor_tensor(qq[:], dd[:], g_pre[:], ALU.mult).then_inc(yb_ready, 1)
                    if c == 15:
                        ky = bass.ds(i * MT + KD, MT)
                        dve.wait_ge(yb_hi, i + 1)
                        v.tensor_tensor(yT[:, ky, 1, :], qq[:], yT[:, ky, 0, :].bitcast(F32), ALU.subtract).then_inc(yb_lo, 1)
                    if c == 15:
                        add_half(ca[:], 1, i * NK + 4, half)
                        freed(3)
                        v.tensor_tensor(cv[:, :, 2:S + 2], ca[:], va[:], ALU.mult).then_inc(cv_ready, 1)
                    if c in (16, 17, 18):
                        k = c - 16
                        if k == 0:
                            dve.wait_ge(cv_ready, i + 1)
                        for m in range(MT):
                            if k == 0:
                                v.tensor_scalar(conv_a[:, m, :], cv[:, m, 0:S], v_("aw0", i * MT + m),
                                                v_("ab", i * MT + m), ALU.mult, ALU.add).then_inc(conv_a_step, 1)
                            else:
                                dve.wait_ge(conv_a_step, i * 6 + MT * (k - 1) + m + 1)
                                v.scalar_tensor_tensor(out=conv_a[:, m, :], in0=cv[:, m, k:k + S],
                                                       scalar=v_(f"aw{k}", i * MT + m), in1=conv_a[:, m, :],
                                                       op0=ALU.mult, op1=ALU.add).then_inc(conv_a_step, 1)
                    if c == 19:
                        add_half(ba[:], 0, i * NK + 5, half)
                        freed(4)
                        dve.wait_ge(conv_a_step, i * 6 + 6)
                        v.tensor_tensor(conv_a[:], conv_a[:], ba[:], ALU.mult).then_inc(ba_conv, 1)
                    if c == 23:
                        dve.wait_ge(half_ready, i * NK + 6)
                        v.tensor_tensor(g_pre[:], acc[:, 1, :, 0:S], half[:], ALU.add).then_inc(acc_freed, 1)
                        freed(5)
                        dve.wait_ge(ba_conv, i + 1)
                        v.tensor_tensor(va[:], conv_a[:], g_pre[:], ALU.mult).then_inc(ga_silu, 1)
                        dve.wait_ge(ga_silu, i + 1)
                        dve.wait_ge(ga_sig, i + 1)
                        v.tensor_tensor(va[:], va[:], g_sig[:], ALU.mult).then_inc(ya_ready, 1)
                        ky = bass.ds(i * MT, MT)
                        dve.wait_ge(ya_hi, i + 1)
                        v.tensor_tensor(yT[:, ky, 1, :], va[:], yT[:, ky, 0, :].bitcast(F32), ALU.subtract).then_inc(ya_lo, 1)
            G0 = PAIRS * NK

            dve.wait_ge(mem_squared, PAIRS * TT)
            v.tensor_reduce(m_s1, m_ss, AX_X, ALU.add).then_inc(mem_stat, 1)
            dve.wait_ge(mem_stat, 1)
            v.tensor_scalar(m_rs, m_s1, 1.0 / D, EPS, ALU.mult, ALU.add).then_inc(mem_stat, 1)
            dve.wait_ge(mem_stat, 3)
            v.reciprocal(m_rs, m_rt).then_inc(mem_stat, 1)
            dve.wait_ge(mem_stat, 4)

            with dve.Fori(0, NG // 2) as i:
                for s in range(2):
                    cols = bass.ds(i * (2 * MW) + s * MW, MW)
                    for q in range(U_GO):
                        c = U_OUT + s * U_GO + q
                        low(i, 2 * U_GO, c + RING)
                        if q == 2:
                            dve.wait_ge(turn_done, i * 8 + KD + 4 * s)
                            for t in range(TT):
                                v.tensor_scalar(stage[:, t, :], memb[:, t, cols], m_rs[:, t:t + 1], None,
                                                ALU.mult).then_inc(mem_staged, 1)
                        if 5 <= q < 9:
                            k = q - 5
                            kc = bass.ds(i * 8 + 4 * s + k, 1)
                            turned_low(xT[:, kc, 1, :].rearrange("p a b -> p (a b)"),
                                       xT[:, kc, 0, :].rearrange("p a b -> p (a b)"),
                                       v_("mem_g", i * 8 + 4 * s + k), i * 8 + KD + 4 * s + k + 1, k)
                        if q == U_GO - 1:
                            dve.wait_ge(units_used, i * (2 * U_GO) + c + 1)
                            v.tensor_tensor(h[:, :, cols], acc[:, s], h[:, :, cols], ALU.add).then_inc(acc_freed, 1)
            G0 += NG

            def sum_half(a, group, halves, hi, lo, before, unit=None):
                add_half(half_k[:], a, halves, half_k)
                if unit is not None:
                    low(*unit)
                dve.wait_ge(acc_freed, group + 3)
                dve.wait_ge(kq_hi, before + 1)
                v.tensor_tensor(lo, half_k[:], hi.bitcast(F32), ALU.subtract).then_inc(kq_lo, 1)

            for c in range(U_KH):
                for k in H_TURNS[c]:
                    turned_low(hT[:, k, 1, :], hT[:, k, 0, :], v_("x_g", k), 2 * KD + k + 1, k % 4)
                low(0, 0, U_K0 + c + RING)
                if c == 6:
                    dve.wait_ge(h_squared, 2 * NG)
                    v.tensor_reduce(h_s1, h_ss, AX_X, ALU.add).then_inc(h_stat, 1)
                    dve.wait_ge(h_stat, 1)
                    v.tensor_scalar(h_rs, h_s1, 1.0 / D, EPS, ALU.mult, ALU.add).then_inc(h_stat, 1)
                if c == 7:
                    dve.wait_ge(h_stat, 3)
                    v.reciprocal(h_rs, h_rt).then_inc(h_stat, 1)
                    dve.wait_ge(h_stat, 4)
                    v.tensor_scalar(h_sc, h_rs, SCORE_SCALE, None, ALU.mult).then_inc(h_stat, 1)
                    dve.wait_ge(h_stat, 5)
                if c % PU == PU - 1:
                    g = c // PU
                    sum_half(g, G0 + g, G0 - NG + g + 1, k_hi[:, 2 * g:2 * g + 2, :], k_lo[:, 2 * g:2 * g + 2, :], g)
            G0 += 2
            H0 = G0 - NG

            def queries_values(i, per, u, groups, halves, head):
                for c in range(U_KH + U_V):
                    low(i, per, u + c + RING)
                    if c in (PU - 1, 2 * PU - 1):
                        g = c // PU
                        sum_half(g, groups + g, halves + g + 1, q_hi[:, 2 * g:2 * g + 2, :],
                                 q_lo[:, 2 * g:2 * g + 2, :], head * 4 + 2 + g)
                    if c == U_KH + 2:
                        dve.wait_ge(scores_done, head + 1)
                        v.tensor_reduce(s_max, aux[:, 0, :].rearrange("p (t m) -> p t m", t=TT), AX_X,
                                        ALU.max).then_inc(score_max, 1)
                        dve.wait_ge(score_max, head * 2 + 1)
                        v.scalar_tensor_tensor(out=s_nmax, in0=s_max, scalar=-1.0, in1=h_sc, op0=ALU.mult,
                                               op1=ALU.mult).then_inc(score_max, 1)
                    if c == U_KH + 3:
                        dve.wait_ge(exp_done, head * 2 + 2)
                        v.reciprocal(s_rsum, s_sum).then_inc(exp_scale, 1)
                        dve.wait_ge(exp_scale, head * 3 + 1)
                        for t in range(TT):
                            v.tensor_scalar(pp[:, t, :], pp[:, t, :], s_rsum[:, t:t + 1], None, ALU.mult).then_inc(exp_scale, 1)
                    if c == U_KH + 6:
                        dve.wait_ge(pt_hi, head + 1)
                        v.tensor_tensor(pT_lo[:].rearrange("p a b -> p (a b)"), aux[:, 1, :],
                                        pT_hi[:].rearrange("p a b -> p (a b)").bitcast(F32), ALU.subtract).then_inc(pt_lo, 1)
                    if c == U_KH + U_V - 1:
                        dve.wait_ge(v_hi_ready, head * TT + TT)
                        v.tensor_tensor(v_lo[:], acc[:, 0], v_hi[:].bitcast(F32), ALU.subtract).then_inc(acc_freed, 1)

            def heads_out(head):
                for b in range(2):
                    kc = slice(head * HC + 2 * b, head * HC + 2 * b + 2) if isinstance(head, int) else bass.ds(head * HC + 2 * b, 2)
                    dve.wait_ge(o_hi, head * 2 + b + 1)
                    v.tensor_tensor(oT[:, kc, 1, :], aux[:, 2 + b, :].rearrange("p (a b) -> p a b", a=2),
                                    oT[:, kc, 0, :].bitcast(F32), ALU.subtract).then_inc(o_lo, 1)

            with dve.Fori(0, HEADS - 1) as i:
                queries_values(i, U_HEAD, U_ATT, i * 5 + G0, i * 4 + H0, i)
                for c in range(U_KH):
                    unit = (i, U_HEAD, U_ATT + U_KH + U_V + c + RING)
                    if c not in (PU - 1, 2 * PU - 1):
                        low(*unit)
                    else:
                        g = c // PU
                        sum_half(1 - g, i * 5 + G0 + 3 + g, i * 4 + H0 + 2 + g + 1, k_hi[:, 2 * g:2 * g + 2, :],
                                 k_lo[:, 2 * g:2 * g + 2, :], i * 4 + 4 + g, unit)
                heads_out(i)
            G0 += 5 * (HEADS - 1)
            H0 += 4 * (HEADS - 1)
            queries_values(0, 0, U_LAST, G0, H0, HEADS - 1)
            for n in range(NG):
                for q in range(U_V):
                    u = U_WO + n * U_V + q
                    if u + RING < U_END:
                        low(0, 0, u + RING)
                    if n == 0 and q == WEIGH_LAST:
                        heads_out(HEADS - 1)
                    if q == U_V - 1 and n < NG - 1:
                        dve.wait_ge(units_used, u + 1)
                        cols = slice(n * MW, (n + 1) * MW)
                        v.tensor_tensor(h[:, :, cols], acc[:, (n + 1) % 2], h[:, :, cols], ALU.add).then_inc(acc_freed, 1)
                        if n == 0:
                            dve.wait_ge(fg_landed, 16)
                        dve.wait_ge(acc_freed, G0 + 3 + n + 3)
                        for t in range(TT):
                            v.tensor_tensor(memb[:, t, cols], h[:, t, cols], fg[:, cols], ALU.mult).then_inc(gained, 1)
            n = NG - 1
            cols = slice(n * MW, D)
            for t in range(TT):
                if t == 0:
                    dve.wait_ge(first_tile, 1)
                else:
                    dve.wait_ge(units_used, U_END)
                v.tensor_tensor(h[:, t, cols], acc[:, (n + 1) % 2, t], h[:, t, cols], ALU.add).then_inc(h_last, 1)
                dve.wait_ge(h_last, t + 1)
                v.tensor_tensor(memb[:, t, cols], h[:, t, cols], fg[:, cols], ALU.mult).then_inc(gained, 1)
                dve.wait_ge(o_squared, n * TT + t + 1)
                v.tensor_reduce(f_s1[:, t:t + 1], f_ss[:, t], AX_X, ALU.add).then_inc(f_stat, 1)
                dve.wait_ge(f_stat, t * 4 + 1)
                v.tensor_scalar(f_ms[:, t:t + 1], f_s1[:, t:t + 1], 1.0 / D, EPS, ALU.mult, ALU.add).then_inc(f_stat, 1)
                dve.wait_ge(f_stat, t * 4 + 3)
                v.reciprocal(f_rs[:, t:t + 1], f_rt[:, t:t + 1]).then_inc(f_stat, 1)
                dve.wait_ge(f_stat, t * 4 + 4)
                dve.wait_ge(gained, n * TT + t + 1)
                for c in range(0, NG, 2):
                    oc = slice(c * MW, (c + 1) * MW)
                    v.tensor_scalar(h[:, t, oc], memb[:, t, oc], f_rs[:, t:t + 1], None, ALU.mult).then_inc(out_dve, 1)


_INS = ['x', 'mem', 'norm_mix_g', 'w_in', 'conv_a_w', 'conv_a_b', 'conv_b_w', 'conv_b_b', 'w_rgate', 'b_rgate',
        'w_igate', 'b_igate', 'lru_lambda', 'w_out', 'norm_x_g', 'norm_mem_g', 'w_q', 'w_kv', 'w_o', 'norm_f_g']


def kernel(**inputs):
    import concourse.bacc as _bacc
    from concourse.bass_utils import run_bass_kernel_spmd as _run

    nc = _bacc.Bacc("TRN2", target_bir_lowering=False, num_devices=1)
    arrays, args = {}, []
    for name in _INS:
        a = np.ascontiguousarray(inputs[name])
        arrays[f"in_{name}_dram"] = a
        args.append(nc.dram_tensor(f"in_{name}_dram", a.shape, mybir.dt.from_np(a.dtype), kind="ExternalInput").ap())
    shape = np.shape(inputs["x"])
    out = nc.dram_tensor("out_0_dram", shape, F32, kind="ExternalOutput").ap()
    hybrid_layer(nc, *args, out)
    r = _run(nc, [arrays], core_ids=[0])
    return r.results[0]["out_0_dram"]
```
